# Optimizing a Trainium2 kernel written in Bass

```python
import jax, jax.numpy as jnp
from jax import lax
import numpy as np

D_MODEL = 1024
BATCH = 1
SEQ = 256
DEPTH = 2

HEAD_DIM = 64
N_HEADS = D_MODEL // HEAD_DIM
N_HEADS_MOBA = N_HEADS // 2
N_HEADS_DIL = N_HEADS - N_HEADS_MOBA
D_MOBA = N_HEADS_MOBA * HEAD_DIM
D_DIL = N_HEADS_DIL * HEAD_DIM
D_FF = 4 * D_MODEL
MOBA_BLOCK = 256
MOBA_TOPK = 3
MOBA_Q_BLOCK = 32
DILATED_CONFIGS = ((128, 1), (512, 4), (2048, 16))
DIL_Q_BLOCK = 64
ROPE_THETA = 10000.0
NORM_EPS = 1e-6
NEG_INF = -1e30

kernel_name = "hymba_moba_dilated_hybrid"

def rms_norm(x, g):
    xf = x.astype(jnp.float32)
    y = xf * lax.rsqrt(jnp.mean(xf * xf, axis=-1, keepdims=True) + NORM_EPS)
    return (y * g.astype(jnp.float32)).astype(x.dtype)

def rope_tables(seq):
    inv = 1.0 / (ROPE_THETA ** (jnp.arange(0, HEAD_DIM, 2, dtype=jnp.float32) / HEAD_DIM))
    ang = jnp.arange(seq, dtype=jnp.float32)[:, None] * inv[None, :]
    return jnp.cos(ang), jnp.sin(ang)

def apply_rope(x, cos, sin):
    x1, x2 = jnp.split(x.astype(jnp.float32), 2, axis=-1)
    out = jnp.concatenate([x1 * cos - x2 * sin, x2 * cos + x1 * sin], axis=-1)
    return out.astype(x.dtype)

def split_heads(t, n_heads):
    b, s, _ = t.shape
    return t.reshape(b, s, n_heads, HEAD_DIM).transpose(0, 2, 1, 3)

def merge_heads(t):
    b, h, s, hd = t.shape
    return t.transpose(0, 2, 1, 3).reshape(b, s, h * hd)

def moba_attention(q, k, v):
    b, h, s, hd = q.shape
    nb = -(-s // MOBA_BLOCK)
    pad = nb * MOBA_BLOCK - s
    k_blocks = jnp.pad(k, ((0, 0), (0, 0), (0, pad), (0, 0))).reshape(b, h, nb, MOBA_BLOCK, hd)
    v_blocks = jnp.pad(v, ((0, 0), (0, 0), (0, pad), (0, 0))).reshape(b, h, nb, MOBA_BLOCK, hd)
    k_mean = jnp.mean(k_blocks.astype(jnp.float32), axis=3)
    q_block_id = jnp.arange(s) // MOBA_BLOCK
    gate = jnp.einsum('bhsd,bhnd->bhsn', q.astype(jnp.float32), k_mean)
    past = jnp.arange(nb)[None, :] < q_block_id[:, None]
    gate = jnp.where(past, gate, NEG_INF)
    topk = min(MOBA_TOPK, nb)
    _, sel = lax.top_k(gate, topk)
    sel_valid = sel < q_block_id[:, None]
    gather_blocks = jax.vmap(jax.vmap(lambda blocks, idx: blocks[idx]))
    scale = HEAD_DIM ** -0.5

    def one_block(start):
        qb = lax.dynamic_slice_in_dim(q, start, MOBA_Q_BLOCK, axis=2)
        selb = lax.dynamic_slice_in_dim(sel, start, MOBA_Q_BLOCK, axis=2)
        validb = lax.dynamic_slice_in_dim(sel_valid, start, MOBA_Q_BLOCK, axis=2)
        t = start + jnp.arange(MOBA_Q_BLOCK)
        own = start // MOBA_BLOCK
        k_own = lax.dynamic_index_in_dim(k_blocks, own, axis=2, keepdims=False)
        v_own = lax.dynamic_index_in_dim(v_blocks, own, axis=2, keepdims=False)
        k_sel = gather_blocks(k_blocks, selb)
        v_sel = gather_blocks(v_blocks, selb)
        s_sel = jnp.einsum('bhqd,bhqkjd->bhqkj', qb, k_sel).astype(jnp.float32) * scale
        s_sel = jnp.where(validb[..., None], s_sel, NEG_INF).reshape(b, h, MOBA_Q_BLOCK, topk * MOBA_BLOCK)
        s_own = jnp.einsum('bhqd,bhjd->bhqj', qb, k_own).astype(jnp.float32) * scale
        own_pos = own * MOBA_BLOCK + jnp.arange(MOBA_BLOCK)
        s_own = jnp.where(own_pos[None, :] <= t[:, None], s_own, NEG_INF)
        p = jax.nn.softmax(jnp.concatenate([s_sel, s_own], axis=-1), axis=-1).astype(v.dtype)
        p_sel = p[..., :topk * MOBA_BLOCK].reshape(b, h, MOBA_Q_BLOCK, topk, MOBA_BLOCK)
        p_own = p[..., topk * MOBA_BLOCK:]
        return (jnp.einsum('bhqkj,bhqkjd->bhqd', p_sel, v_sel)
                + jnp.einsum('bhqj,bhjd->bhqd', p_own, v_own))

    starts = jnp.arange(s // MOBA_Q_BLOCK) * MOBA_Q_BLOCK
    out = lax.map(one_block, starts)
    return jnp.moveaxis(out, 0, 2).reshape(b, h, s, hd)

def dilated_attention(q, k, v):
    b, h, s, hd = q.shape
    scale = HEAD_DIM ** -0.5

    def one_block(start):
        qb = lax.dynamic_slice_in_dim(q, start, DIL_Q_BLOCK, axis=2)
        t = start + jnp.arange(DIL_Q_BLOCK)
        outs, lses = [], []
        for window, dilation in DILATED_CONFIGS:
            n_keys = window // dilation + 1
            idx = t[:, None] - dilation * jnp.arange(n_keys)[None, :]
            valid = idx >= 0
            idx = jnp.maximum(idx, 0)
            kg = jnp.take(k, idx, axis=2)
            vg = jnp.take(v, idx, axis=2)
            sc = jnp.einsum('bhqd,bhqnd->bhqn', qb, kg).astype(jnp.float32) * scale
            sc = jnp.where(valid, sc, NEG_INF)
            lse = jax.nn.logsumexp(sc, axis=-1)
            p = jnp.exp(sc - lse[..., None])
            outs.append(jnp.einsum('bhqn,bhqnd->bhqd', p, vg.astype(jnp.float32)))
            lses.append(lse)
        w = jax.nn.softmax(jnp.stack(lses, axis=0), axis=0)
        out = jnp.einsum('gbhq,gbhqd->bhqd', w, jnp.stack(outs, axis=0))
        return out.astype(v.dtype)

    starts = jnp.arange(s // DIL_Q_BLOCK) * DIL_Q_BLOCK
    out = lax.map(one_block, starts)
    return jnp.moveaxis(out, 0, 2).reshape(b, h, s, hd)

def hybrid_layer(x, attn_norm, w_in, moba_out_norm, dil_out_norm, w_out,
                 mlp_norm, w_up, w_down, cos, sin):
    h = rms_norm(x, attn_norm)
    proj = h @ w_in
    qa, ka, va, qd, kd, vd = jnp.split(
        proj, [D_MOBA, 2 * D_MOBA, 3 * D_MOBA, 3 * D_MOBA + D_DIL, 3 * D_MOBA + 2 * D_DIL], axis=-1)
    qa = apply_rope(split_heads(qa, N_HEADS_MOBA), cos, sin)
    ka = apply_rope(split_heads(ka, N_HEADS_MOBA), cos, sin)
    va = split_heads(va, N_HEADS_MOBA)
    qd = apply_rope(split_heads(qd, N_HEADS_DIL), cos, sin)
    kd = apply_rope(split_heads(kd, N_HEADS_DIL), cos, sin)
    vd = split_heads(vd, N_HEADS_DIL)
    out_a = rms_norm(merge_heads(moba_attention(qa, ka, va)), moba_out_norm)
    out_d = rms_norm(merge_heads(dilated_attention(qd, kd, vd)), dil_out_norm)
    x = x + jnp.concatenate([out_a, out_d], axis=-1) @ w_out
    h = rms_norm(x, mlp_norm)
    x = x + jnp.square(jax.nn.relu(h @ w_up)) @ w_down
    return x

def setup_inputs(seed: int = 0) -> dict:
    key = jax.random.key(seed)
    ks = jax.random.split(key, 10)
    f32 = jnp.float32
    return {
        "x": jax.random.normal(ks[0], (BATCH, SEQ, D_MODEL), f32),
        "attn_norm": 1.0 + 0.02 * jax.random.normal(ks[1], (DEPTH, D_MODEL), f32),
        "w_in": jax.random.normal(ks[2], (DEPTH, D_MODEL, 3 * D_MODEL), f32) * D_MODEL ** -0.5,
        "moba_out_norm": 1.0 + 0.02 * jax.random.normal(ks[3], (DEPTH, D_MOBA), f32),
        "dil_out_norm": 1.0 + 0.02 * jax.random.normal(ks[4], (DEPTH, D_DIL), f32),
        "w_out": jax.random.normal(ks[5], (DEPTH, D_MODEL, D_MODEL), f32) * (2 * D_MODEL) ** -0.5,
        "mlp_norm": 1.0 + 0.02 * jax.random.normal(ks[6], (DEPTH, D_MODEL), f32),
        "w_up": jax.random.normal(ks[7], (DEPTH, D_MODEL, D_FF), f32) * D_MODEL ** -0.5,
        "w_down": jax.random.normal(ks[8], (DEPTH, D_FF, D_MODEL), f32) * D_FF ** -0.5,
        "final_norm": 1.0 + 0.02 * jax.random.normal(ks[9], (D_MODEL,), f32),
    }

def reference(x, attn_norm, w_in, moba_out_norm, dil_out_norm, w_out,
              mlp_norm, w_up, w_down, final_norm):
    cos, sin = rope_tables(x.shape[1])
    for l in range(DEPTH):
        x = hybrid_layer(x, attn_norm[l], w_in[l], moba_out_norm[l], dil_out_norm[l], w_out[l],
                         mlp_norm[l], w_up[l], w_down[l], cos, sin)
    return rms_norm(x, final_norm)


_drawn_inputs = setup_inputs


def setup_inputs(seed=0):
    import zlib

    import numpy as np

    out = dict(_drawn_inputs(seed))
    spreads = {}
    factors = {}
    for name, (base, spread) in spreads.items():
        noise = np.random.default_rng([zlib.crc32(name.encode()), seed]).standard_normal(out[name].shape)
        drawn = base * np.exp(spread * noise) if base else spread * noise
        out[name] = __import__('jax').numpy.asarray(drawn.astype(out[name].dtype))
    for name, factor in factors.items():
        out[name] = (out[name] * factor).astype(out[name].dtype)
    return out
```

```python
import math

import numpy as np

import concourse.bass as bass
from concourse import mybir
from contextlib import ExitStack

F32 = mybir.dt.float32
F32R = mybir.dt.float32r
BF16 = mybir.dt.bfloat16
ALU = mybir.AluOpType
ACT = mybir.ActivationFunctionType

P = 128
D_MODEL = 1024
SEQ = 256
DEPTH = 2
HEAD_DIM = 64
HALF = HEAD_DIM // 2
N_HEADS = D_MODEL // HEAD_DIM
SET_HEADS = N_HEADS // 2
D_SET = SET_HEADS * HEAD_DIM
D_FF = 4 * D_MODEL
SCALE = HEAD_DIM ** -0.5
DILATED_CONFIGS = ((128, 1), (512, 4), (2048, 16))
ROPE_THETA = 10000.0
NORM_EPS = 1e-6
NEG_INF = -1e30

TOK = SEQ // P
KT = D_MODEL // P
BANK = 512

CHUNK = 2048
UNIT = CHUNK // 2
RING = 4
UNITS_HELD = 2 * RING
GROUPS = 3 * D_MODEL // BANK
IN_CHUNKS = 2 * GROUPS
OUT_CHUNKS = D_MODEL * D_MODEL // (P * CHUNK)
ATT_UNITS = 2 * (IN_CHUNKS + OUT_CHUNKS)
UPS = D_FF // BANK * 2
CHUNKS = IN_CHUNKS + OUT_CHUNKS + 2 * UPS
UNITS = 2 * CHUNKS
FIRST_UP = IN_CHUNKS + OUT_CHUNKS
HI_AHEAD = 6
LO_AHEAD = 4
VISITS = CHUNKS // RING
MLP_TURNS = (UPS - 2) // 2
SPLIT_TURNS = MLP_TURNS - 1

GROUP_COLUMNS = [3, 4, 5, 0, 1, 2]
ROPE_GROUPS = {0: 0, 1: 1, 3: 2, 4: 3}
V_GROUPS = {2: 0, 5: 1}

QK_AT = {23 + 2 * h if h < 8 else 38 + h: h for h in range(N_HEADS)}
PT_AT = {s + 2: h for s, h in QK_AT.items()}
PV_AT = {s + 3: h for s, h in QK_AT.items()}
QKT_AT = {12: 0, 13: 1, 20: 2, 21: 3, 38: 4, 40: 5, 43: 6, 44: 7}
ROPE_AT = {8 * g + 8: g for g in ROPE_GROUPS}
V_AT = {8 * g + 8: g for g in V_GROUPS}
TAIL = 56
O_AT = {min(s + 1, TAIL): h // 4 for s, h in PV_AT.items() if h % 4 == 3}
TURN_D, TURN_A = 42, 54
X_AT = {58 + n: n for n in range(2 * TOK)}

TR_X, TR_D, TR_A, TR_M, TRS = 0, 4, 6, 8, 12
ST_X, ST_D, ST_A, ST_M, STATS = 0, 1, 2, 3, 4


def hybrid_kernel(nc, x_d, w_in, w_out, w_up, w_down, final_g, gain_rows_d, ident_d, masks_d, rope_d,
                  out_d):
    ctx = ExitStack()
    with ctx:
        def sb(name, shape, dt=F32):
            return ctx.enter_context(nc.sbuf_tensor(name, [P, *shape], dt))

        def sem(name):
            return ctx.enter_context(nc.semaphore(name))

        raw = sb("raw", [RING, CHUNK])
        w_hi = sb("w_hi", [RING, CHUNK], F32R)
        w_lo = sb("w_lo", [RING, CHUNK], F32R)
        x = sb("x", [TOK, D_MODEL])
        xt_hi = sb("xt_hi", [KT, SEQ], F32R)
        xt_lo = sb("xt_lo", [KT, SEQ], F32R)
        ot_hi = sb("ot_hi", [KT, SEQ], F32R)
        ot_lo = sb("ot_lo", [KT, SEQ], F32R)
        squares = sb("squares", [TOK, D_MODEL], BF16)
        rope_a = sb("rope_a", [TOK, D_SET])
        rope_b = sb("rope_b", [TOK, D_SET])
        roped = sb("roped", [2, TOK, D_SET])
        v = sb("v", [2, TOK, D_SET])
        q_t = sb("q_t", [4, SEQ])
        k_t = sb("k_t", [4, SEQ])
        scores = sb("scores", [2, 3 * P])
        probs = sb("probs", [2, 3 * P])
        probs_t = sb("probs_t", [2, 3 * P])
        row_max = sb("row_max", [2, TOK])
        row_bias = sb("row_bias", [2, TOK])
        row_sum = sb("row_sum", [TOK, N_HEADS])
        row_inv = sb("row_inv", [TOK, N_HEADS])
        o = sb("o", [TOK, D_SET])
        up_relu = sb("up_relu", [2 * SEQ])
        up_sq = sb("up_sq", [2 * SEQ])
        h_hi = sb("h_hi", [2, 2, SEQ], F32R)
        h_lo = sb("h_lo", [2, 2, SEQ], F32R)
        masks = sb("masks", [2, 2 * P])
        ident = sb("ident", [P])
        rope_tab = sb("rope_tab", [TOK, 3 * HALF])
        rope_r = sb("rope_r", [TOK, 3 * HALF])
        n_gains = DEPTH * (2 * KT + 2 * 4)
        gain_rows = ctx.enter_context(nc.sbuf_tensor("gain_rows", [n_gains, P], F32))
        gains_all = sb("gains_all", [n_gains])
        gains = sb("gains", [2 * KT + 2 * 4])
        final_gain = sb("final_gain", [D_MODEL])
        sums = sb("sums", [STATS, TOK])
        means = sb("means", [STATS, TOK])
        rstd = sb("rstd", [STATS, TOK])
        powers = sb("powers", [2, TOK])

        banks = [ctx.enter_context(nc.psum_tensor(f"bank{n}", [P, BANK], F32)) for n in range(8)]
        s_banks, t_bank, o_bank = banks[4:6], banks[6], banks[7]
        acc_d = [[banks[2 * t + n] for n in range(2)] for t in range(TOK)]
        acc_a = [[banks[4], banks[6]], [banks[5], banks[7]]]

        x_loaded = sem("x_loaded")
        masks_loaded = sem("masks_loaded")
        gains_loaded = sem("gains_loaded")
        rope_loaded = sem("rope_loaded")
        final_gain_loaded = sem("final_gain_loaded")
        powers_set = sem("powers_set")
        gains_turned = sem("gains_turned")
        gains_kept = sem("gains_kept")
        raw_ready = [sem(f"raw_ready{n}") for n in range(RING)]
        hi_done = sem("hi_done")
        split_done = sem("split_done")
        weights_used = sem("weights_used")
        x_updated = sem("x_updated")
        x_mid = sem("x_mid")
        x_d_added = sem("x_d_added")
        turned = sem("turned")
        turned_hi = sem("turned_hi")
        turned_lo = sem("turned_lo")
        summed = sem("summed")
        mean_done = sem("mean_done")
        rstd_done = sem("rstd_done")
        rope_scaled = sem("rope_scaled")
        gains_done = sem("gains_done")
        rope_terms = sem("rope_terms")
        rope_done = sem("rope_done")
        v_done = sem("v_done")
        qk_turned = sem("qk_turned")
        qk_copied = sem("qk_copied")
        scored = sem("scored")
        masked = sem("masked")
        bias_done = sem("bias_done")
        exp_done = sem("exp_done")
        p_turned = sem("p_turned")
        p_copied = sem("p_copied")
        pv_done = sem("pv_done")
        inv_done = sem("inv_done")
        o_done = sem("o_done")
        acc_a_half = sem("acc_a_half")
        acc_mlp_half = sem("acc_mlp_half")
        relu_done = sem("relu_done")
        h_done = sem("h_done")
        h_hi_done = sem("h_hi_done")
        h_split = sem("h_split")
        x_gained = sem("x_gained")
        final_0 = sem("final_0")
        final_1 = sem("final_1")
        out_written = sem("out_written")

        block = ctx.enter_context(nc.Block())

        in_v = w_in.rearrange("l (k p) n -> l p k n", p=P)
        out_v = w_out.rearrange("l (k p) n -> l p k n", p=P)
        up_v = w_up.rearrange("l (k p) n -> l p k n", p=P)
        down_v = w_down.rearrange("l (k p) n -> l p k n", p=P)

        def used(l, u):
            return l * UNITS + u + (1 + UNITS_HELD)

        def visit(l, c):
            return l * (16 * VISITS) + 16 * (c // RING + 1)

        def wait_all(eng, constant, *others):
            values = [eng.compute_val(value) for _, value in others]
            eng.wait_ge(*constant)
            for (other, _), value in zip(others, values):
                eng.wait_ge(other, value)

        @block.sync
        def _(sp):
            x_v = x_d[0].rearrange("(t p) n -> t p n", p=P)
            sp.dma_start(ident[:, :], ident_d).then_inc(gains_loaded, 16)
            for t in range(TOK):
                sp.dma_start(x[:, t, :], x_v[t]).then_inc(x_loaded, 16)

            def load(l, c, slot, src, k):
                wait_all(sp, (split_done, UNITS_HELD), (split_done, l * UNITS + c * 2 + 2))
                sp.dma_start(raw[:, slot, :].rearrange("p (k n) -> p k n", k=k), src)\
                    .then_inc(raw_ready[slot], 16)

            def at(view, l):
                return view[bass.ds(l, 1)].rearrange("a p k n -> p (a k) n")

            with sp.Fori(0, DEPTH) as l:
                for c in range(IN_CHUNKS):
                    cols = GROUP_COLUMNS[c // 2] * BANK
                    load(l, c, c % RING, at(in_v[:, :, 4 * (c % 2):4 * (c % 2) + 4, cols:cols + BANK], l), 4)
                for n in range(OUT_CHUNKS):
                    c = IN_CHUNKS + n
                    k = 2 * ((n + 2) % OUT_CHUNKS)
                    load(l, c, c % RING, at(out_v[:, :, k:k + 2, :], l), 2)

                def load_up(l, c, i, slot):
                    src = up_v[bass.ds(l, 1), :, :, bass.ds(i * SEQ, SEQ)]
                    load(l, c, slot, src.rearrange("a p k n -> p (a k) n"), KT)

                def load_down(l, c, i, slot):
                    src = down_v[bass.ds(l, 1), :, bass.ds(i * 2, 2), :]
                    load(l, c, slot, src.rearrange("a p k n -> p (a k) n"), 2)

                load_up(l, FIRST_UP, 0, FIRST_UP % RING)
                with sp.Fori(0, MLP_TURNS) as j:
                    c = j * 4 + (FIRST_UP + 1)
                    load_up(l, c, j * 2 + 1, 1)
                    load_down(l, c + 1, j * 2, 2)
                    load_up(l, c + 2, j * 2 + 2, 3)
                    load_down(l, c + 3, j * 2 + 1, 0)
                load_up(l, CHUNKS - 3, UPS - 1, 1)
                load_down(l, CHUNKS - 2, UPS - 2, 2)
                load_down(l, CHUNKS - 1, UPS - 1, 3)

            sp.dma_start(final_gain[:, :], final_g.rearrange("(a n) -> a n", a=1).broadcast_to([P, D_MODEL]))\
                .then_inc(final_gain_loaded, 16)
            for n in range(2):
                cols = slice(n * BANK, (n + 1) * BANK)
                sp.wait_ge(final_0, n + 1)
                sp.dma_start(out_d[0][0:P, cols], x[:, 0, cols]).then_inc(out_written, 16)
            sp.wait_ge(out_written, 16 * 4)

        @block.gpsimd
        def _(pool):
            pool.memset(powers[:, 0, :], -0.5).then_inc(powers_set, 1)
            pool.memset(powers[:, 1, :], -1.0).then_inc(powers_set, 1)

            def inverse_rms(l, n, width):
                wait_all(pool, (powers_set, 2), (summed, l * STATS + n + 2))
                pool.tensor_scalar(means[:, n, :], sums[:, n, :], 1.0 / width, NORM_EPS,
                                   ALU.mult, ALU.add).then_inc(mean_done, 1)
                pool.wait_ge(mean_done, l * STATS + n + 1)
                pool.tensor_tensor(rstd[:, n, :], means[:, n, :], powers[:, int(n == ST_M), :],
                                   ALU.pow).then_inc(rstd_done, 1)

            def rope_sum(l, j, t):
                pool.wait_ge(rope_terms, l * 8 + 2 * j + t + 1)
                if t == 0:
                    pool.wait_ge(qk_turned, l * 8 + 2 * j + 2)
                pool.tensor_tensor(roped[:, j % 2, t, :], rope_a[:, t, :], rope_b[:, t, :], ALU.add)\
                    .then_inc(rope_done, 1)

            with pool.Fori(0, DEPTH) as l:
                inverse_rms(l, ST_X, D_MODEL)
                wait_all(pool, (rope_loaded, 16), (rstd_done, l * STATS + ST_X + 1))
                for t in range(TOK):
                    last = pool.tensor_scalar(rope_r[:, t, :], rope_tab[:, t, :],
                                              rstd[:, ST_X, t:t + 1], None, ALU.mult)
                last.then_inc(rope_scaled, 1)
                for j in range(4):
                    for t in range(TOK):
                        rope_sum(l, j, t)
                inverse_rms(l, ST_D, D_SET)
                inverse_rms(l, ST_A, D_SET)
                inverse_rms(l, ST_M, D_MODEL)
            pool.wait_ge(mean_done, DEPTH * STATS + 1)
            pool.tensor_tensor(rstd[:, ST_X, :], means[:, ST_X, :], powers[:, 0, :], ALU.pow)\
                .then_inc(rstd_done, 1)

        @block.scalar
        def _(act):
            act.dma_start(gain_rows[:, :], gain_rows_d).then_inc(gains_loaded, 16)
            act.dma_start(rope_tab[:, :, :], rope_d).then_inc(rope_loaded, 16)
            act.dma_start(masks[:, :, :], masks_d).then_inc(masks_loaded, 16)
            act.sem_inc(qk_copied, 1)
            act.sem_inc(p_copied, 1)
            act.sem_inc(exp_done, 2)

            def hi(l, c, slot, half, seen):
                if half == 0:
                    act.wait_ge(raw_ready[slot], seen)
                act.wait_ge(weights_used, l * UNITS + c * 2 + (half + 1))
                part = slice(half * UNIT, (half + 1) * UNIT)
                act.copy(w_hi[:, slot, part], raw[:, slot, part]).then_inc(hi_done, 1)

            def turned_to_hi(l, n, bank, dst, k0, gain0):
                act.wait_ge(turned, l * TRS + n + 1)
                if n == 0:
                    act.wait_ge(gains_done, l + 1)
                for k in range(2):
                    last = act.activation(dst[:, k0 + k, :], bank[:, k * SEQ:(k + 1) * SEQ], ACT.Copy,
                                          scale=gains[:, gain0 + k:gain0 + k + 1])
                last.then_inc(turned_hi, 1)

            def square_sums(l, n, src, width):
                act.wait_ge(summed, l * STATS + n + 1)
                for t in range(TOK):
                    last = act.activation(squares[:, t, 0:width], src[:, t, :], ACT.Square,
                                          accum_out=sums[:, n, t:t + 1])
                last.then_inc(summed, 1)

            act.sem_inc(summed, 1)

            with act.Fori(0, DEPTH) as l:
                for u in range(HI_AHEAD):
                    if u < 4:
                        turned_to_hi(l, TR_X + u, banks[4 + u], xt_hi, 2 * u, 2 * u)
                    hi(l, u // 2, u // 2 % RING, u % 2, visit(l, u // 2))
                square_sums(l, ST_X, x, D_MODEL)
                for s in range(2 * ATT_UNITS):
                    u = s // 2 + HI_AHEAD
                    if s in V_AT:
                        g = V_AT[s]
                        act.wait_ge(weights_used, used(l, 4 * g + 3))
                        act.wait_ge(rstd_done, l * STATS + ST_X + 1)
                        for t in range(TOK):
                            last = act.activation(v[:, V_GROUPS[g], t, :], banks[2 * (g % 2) + t][:, :],
                                                  ACT.Copy, scale=rstd[:, ST_X, t:t + 1])
                        last.then_inc(v_done, 1)
                    if s in QKT_AT:
                        n = QKT_AT[s]
                        dst = (q_t, k_t)[n // 2 % 2]
                        act.wait_ge(qk_turned, l * 8 + n + 5)
                        act.copy(dst[:, 2 * (n % 2):2 * (n % 2) + 2, :],
                                 t_bank[:, :].rearrange("p (a b) -> p a b", a=2)).then_inc(qk_copied, 1)
                    if s in PT_AT:
                        h = PT_AT[s]
                        act.wait_ge(p_turned, l * N_HEADS + h + 3)
                        act.wait_ge(pv_done, l * N_HEADS + h + 1)
                        act.copy(probs_t[:, h % 2, :], t_bank[:, 0:3 * P]).then_inc(p_copied, 1)
                    if s in QK_AT:
                        h = QK_AT[s]
                        act.wait_ge(bias_done, l * N_HEADS + h + 1)
                        act.wait_ge(p_turned, l * N_HEADS + h + 1)
                        for t in range(TOK):
                            cols = slice(0, P) if t == 0 else slice(P, 3 * P)
                            last = act.activation(probs[:, h % 2, cols], scores[:, h % 2, cols], ACT.Exp,
                                                  scale=SCALE, bias=row_bias[:, h % 2, t:t + 1],
                                                  accum_out=row_sum[:, t, h:h + 1])
                        last.then_inc(exp_done, 1)
                    if s == TURN_D:
                        for n in range(2):
                            turned_to_hi(l, TR_D + n, s_banks[n], ot_hi, 2 * n, 2 * KT + 4 + 2 * n)
                        square_sums(l, ST_D, o, D_SET)
                    if s == TURN_A:
                        turned_to_hi(l, TR_A, s_banks[0], ot_hi, 4, 2 * KT)
                    if s == TAIL:
                        turned_to_hi(l, TR_A + 1, s_banks[1], ot_hi, 6, 2 * KT + 2)
                        square_sums(l, ST_A, o, D_SET)
                    if s % 2 == 0 and u < 2 * (FIRST_UP + 2):
                        hi(l, u // 2, u // 2 % RING, u % 2, visit(l, u // 2))
                for n in range(4):
                    turned_to_hi(l, TR_M + n, banks[n], xt_hi, 2 * n, KT + 2 * n)
                square_sums(l, ST_M, x, D_MODEL)

                def h_to_hi(l, i, b):
                    act.wait_ge(h_done, l * UPS + i + 1)
                    act.wait_ge(weights_used, used(l, i * 4 + (2 * (FIRST_UP - 2) + 1)))
                    act.copy(h_hi[:, b, :, :], up_sq[:, :].rearrange("p (a b) -> p a b", a=2))\
                        .then_inc(h_hi_done, 1)

                def hi_chunk(l, c, slot, seen):
                    for half in range(2):
                        hi(l, c, slot, half, seen)

                hi_chunk(l, FIRST_UP + 2, (FIRST_UP + 2) % RING, visit(l, FIRST_UP + 2))
                h_to_hi(l, 0, 0)
                for c in (FIRST_UP + 3, FIRST_UP + 4):
                    hi_chunk(l, c, c % RING, visit(l, c))
                with act.Fori(0, SPLIT_TURNS) as j:
                    for b in range(2):
                        h_to_hi(l, j * 2 + (1 + b), (1 + b) % 2)
                        for c in (FIRST_UP + 5 + 2 * b, FIRST_UP + 6 + 2 * b):
                            hi_chunk(l, j * 4 + c, c % RING, visit(l, c) + j * 16)
                h_to_hi(l, UPS - 3, 1)
                for c in (CHUNKS - 3, CHUNKS - 2):
                    hi_chunk(l, c, c % RING, visit(l, c))
                h_to_hi(l, UPS - 2, 0)
                hi_chunk(l, CHUNKS - 1, (CHUNKS - 1) % RING, visit(l, CHUNKS - 1))
                h_to_hi(l, UPS - 1, 1)
            for n in range(2):
                act.wait_ge(x_updated, 2 * TOK * DEPTH + 2 * (n + 1))
                act.wait_ge(summed, DEPTH * STATS + n + 1)
                for t in range(TOK):
                    last = act.activation(squares[:, t, n * BANK:(n + 1) * BANK],
                                          x[:, t, n * BANK:(n + 1) * BANK], ACT.Square,
                                          scale=D_MODEL ** -0.5, accum_out=sums[:, n, t:t + 1])
                last.then_inc(summed, 1)
            t = 1
            act.wait_ge(rstd_done, DEPTH * STATS + 1)
            act.wait_ge(x_gained, 2)
            for n in range(2):
                act.activation(x[:, t, n * BANK:(n + 1) * BANK], (rope_a, rope_b)[n][:, t, :], ACT.Copy,
                               scale=rstd[:, ST_X, t:t + 1]).then_inc(final_1, 1)
                act.wait_ge(final_1, n + 1)
                act.dma_start(out_d[0][t * P:(t + 1) * P, n * BANK:(n + 1) * BANK],
                              x[:, t, n * BANK:(n + 1) * BANK]).then_inc(out_written, 16)

        @block.vector
        def _(dve):
            dve.sem_inc(split_done, UNITS_HELD)
            dve.sem_inc(x_updated, 2 * TOK)

            def lo(l, c, slot, half):
                dve.wait_ge(hi_done, l * UNITS + c * 2 + (half + 1))
                part = slice(half * UNIT, (half + 1) * UNIT)
                dve.tensor_tensor(w_lo[:, slot, part], raw[:, slot, part],
                                  w_hi[:, slot, part].bitcast(F32), ALU.subtract).then_inc(split_done, 1)

            def turned_to_lo(l, n, bank, hi_t, lo_t, k0, gain0):
                dve.wait_ge(turned_hi, l * TRS + n + 1)
                for k in range(2):
                    last = dve.scalar_tensor_tensor(
                        out=lo_t[:, k0 + k, :], in0=bank[:, k * SEQ:(k + 1) * SEQ],
                        scalar=gains[:, gain0 + k:gain0 + k + 1], in1=hi_t[:, k0 + k, :].bitcast(F32),
                        op0=ALU.mult, op1=ALU.subtract)
                last.then_inc(turned_lo, 1)

            def add_to_x(bank, t, n, stat, done):
                part = x[:, t, n * BANK:(n + 1) * BANK]
                dve.scalar_tensor_tensor(out=part, in0=bank[:, :], scalar=rstd[:, stat, t:t + 1], in1=part,
                                         op0=ALU.mult, op1=ALU.add).then_inc(done, 1)

            def rope_products(l, g, t):
                j = ROPE_GROUPS[g]
                dve.wait_ge(weights_used, used(l, 4 * g + 3))
                dve.wait_ge(rope_scaled, l + 1)
                if j > 0:
                    dve.wait_ge(rope_done, l * 8 + 2 * (j - 1) + t + 1)
                bank = banks[2 * (g % 2) + t]
                cos, sin, neg = (rope_r[:, t, n * HALF:(n + 1) * HALF] for n in range(3))

                def wide(table, n):
                    return table.unsqueeze(1).broadcast_to([P, n, HALF])

                halves = bank[:, :].rearrange("p (a c) -> p a c", c=HALF)
                dve.tensor_tensor(rope_a[:, t, :].rearrange("p (a c) -> p a c", c=HALF), halves,
                                  wide(cos, 2 * SET_HEADS), ALU.mult)
                b = rope_b[:, t, :].rearrange("p (a c) -> p a c", c=HALF)
                dve.tensor_tensor(b[:, 0::2, :], halves[:, 1::2, :], wide(neg, SET_HEADS), ALU.mult)
                dve.tensor_tensor(b[:, 1::2, :], halves[:, 0::2, :], wide(sin, SET_HEADS), ALU.mult)\
                    .then_inc(rope_terms, 1)

            dve.wait_ge(gains_turned, 1)
            dve.tensor_copy(gains_all[:, :], banks[0][:, 0:n_gains]).then_inc(gains_kept, 1)
            dve.wait_ge(gains_kept, 1)

            with dve.Fori(0, DEPTH) as l:
                at = 0
                to = 0
                for n in (KT, KT, 4, 4):
                    last = dve.tensor_copy(gains[:, to:to + n], gains_all[:, bass.ds(l * n + at, n)])
                    at += DEPTH * n
                    to += n
                last.then_inc(gains_done, 1)
                dve.wait_ge(gains_done, l + 1)
                for n in range(4):
                    turned_to_lo(l, TR_X + n, banks[4 + n], xt_hi, xt_lo, 2 * n, 2 * n)
                    lo(l, n // 2, n // 2 % RING, n % 2)
                for s in range(2 * ATT_UNITS):
                    u = s // 2 + LO_AHEAD
                    if s in O_AT:
                        four = O_AT[s]
                        heads = slice(4 * four, 4 * four + 4)
                        dve.wait_ge(pv_done, l * N_HEADS + 4 * four + 4 + 2)
                        dve.reciprocal(row_inv[:, :, heads], row_sum[:, :, heads]).then_inc(inv_done, 1)
                        dve.wait_ge(inv_done, l * 4 + four + 1)
                        if four == 2:
                            dve.wait_ge(summed, l * STATS + ST_D + 2)
                        cols = four % 2 * 4 * HEAD_DIM
                        for t in range(TOK):
                            last = dve.tensor_tensor(
                                o[:, t, cols:cols + 4 * HEAD_DIM].rearrange("p (h d) -> p h d", h=4),
                                o_bank[:, t * 4 * HEAD_DIM:(t + 1) * 4 * HEAD_DIM].rearrange("p (h d) -> p h d", h=4),
                                row_inv[:, t, heads].unsqueeze(2).broadcast_to([P, 4, HEAD_DIM]), ALU.mult)
                        last.then_inc(o_done, 1)
                    if s in QK_AT:
                        h = QK_AT[s]
                        m = masks[:, h // SET_HEADS, :]
                        wait_all(dve, (masks_loaded, 16), (scored, l * N_HEADS + h + 1),
                                 (exp_done, l * N_HEADS + h + 1))
                        bank = s_banks[h % 2]
                        dve.tensor_tensor_reduce(out=scores[:, h % 2, 0:P], in0=bank[:, 0:P], in1=m[:, P:2 * P],
                                                 scale=1.0, scalar=-3.0e38, op0=ALU.add, op1=ALU.max,
                                                 accum_out=row_max[:, h % 2, 0:1])
                        dve.tensor_tensor_reduce(out=scores[:, h % 2, P:3 * P], in0=bank[:, P:3 * P], in1=m,
                                                 scale=1.0, scalar=-3.0e38, op0=ALU.add, op1=ALU.max,
                                                 accum_out=row_max[:, h % 2, 1:2]).then_inc(masked, 1)
                        dve.wait_ge(masked, l * N_HEADS + h + 1)
                        dve.tensor_scalar(row_bias[:, h % 2, :], row_max[:, h % 2, :], -SCALE, None, ALU.mult)\
                            .then_inc(bias_done, 1)
                    if s in ROPE_AT:
                        for t in range(TOK):
                            rope_products(l, ROPE_AT[s], t)
                    if s == TURN_D:
                        for n in range(2):
                            turned_to_lo(l, TR_D + n, s_banks[n], ot_hi, ot_lo, 2 * n, 2 * KT + 4 + 2 * n)
                    if s == TURN_A:
                        turned_to_lo(l, TR_A, s_banks[0], ot_hi, ot_lo, 4, 2 * KT)
                    if s == TAIL:
                        turned_to_lo(l, TR_A + 1, s_banks[1], ot_hi, ot_lo, 6, 2 * KT + 2)
                    if s in X_AT:
                        n, t = divmod(X_AT[s], TOK)
                        if X_AT[s] == 0:
                            dve.wait_ge(weights_used, used(l, 2 * IN_CHUNKS + 3))
                            dve.wait_ge(rstd_done, l * STATS + ST_D + 1)
                        add_to_x(acc_d[t][n], t, n, ST_D, x_d_added)
                    if s % 2 == 1:
                        lo(l, u // 2, u // 2 % RING, u % 2)
                dve.wait_ge(rstd_done, l * STATS + ST_A + 1)
                dve.wait_ge(x_d_added, l * 4 + 4)
                for n in range(2):
                    if n == 0:
                        dve.wait_ge(acc_a_half, l + 1)
                    else:
                        dve.wait_ge(weights_used, used(l, ATT_UNITS - 1))
                    for t in range(TOK):
                        add_to_x(acc_a[t][n], t, n, ST_A, x_mid)
                for n in range(4):
                    turned_to_lo(l, TR_M + n, banks[n], xt_hi, xt_lo, 2 * n, KT + 2 * n)

                def square_relu(l, i, bank, c):
                    dve.wait_ge(weights_used, used(l, c * 2 + 1))
                    dve.tensor_scalar(up_relu[:, :], bank[:, :], 0.0, None, ALU.max).then_inc(relu_done, 1)
                    dve.wait_ge(relu_done, l * UPS + i + 1)
                    dve.tensor_tensor(up_sq[:, :], up_relu[:, :], up_relu[:, :], ALU.mult).then_inc(h_done, 1)

                def h_to_lo(l, i, b):
                    dve.wait_ge(h_hi_done, l * UPS + i + 1)
                    dve.tensor_tensor(h_lo[:, b, :, :], up_sq[:, :].rearrange("p (a b) -> p a b", a=2),
                                      h_hi[:, b, :, :].bitcast(F32), ALU.subtract).then_inc(h_split, 1)

                def lo_chunk(l, c, slot):
                    for half in range(2):
                        lo(l, c, slot, half)

                def slice_and_split(l, i, b, c_up, c, slot):
                    square_relu(l, i, banks[4 + b], c_up)
                    lo(l, c, slot, 0)
                    h_to_lo(l, i, b)
                    lo(l, c, slot, 1)

                lo_chunk(l, FIRST_UP + 2, (FIRST_UP + 2) % RING)
                slice_and_split(l, 0, 0, FIRST_UP, FIRST_UP + 3, (FIRST_UP + 3) % RING)
                lo_chunk(l, FIRST_UP + 4, (FIRST_UP + 4) % RING)
                with dve.Fori(0, SPLIT_TURNS) as j:
                    for b in range(2):
                        c = FIRST_UP + 5 + 2 * b
                        slice_and_split(l, j * 2 + (1 + b), (1 + b) % 2, j * 4 + (c - 4), j * 4 + c, c % RING)
                        lo_chunk(l, j * 4 + (c + 1), (c + 1) % RING)
                slice_and_split(l, UPS - 3, 1, CHUNKS - 7, CHUNKS - 3, (CHUNKS - 3) % RING)
                lo_chunk(l, CHUNKS - 2, (CHUNKS - 2) % RING)
                slice_and_split(l, UPS - 2, 0, CHUNKS - 5, CHUNKS - 1, (CHUNKS - 1) % RING)
                square_relu(l, UPS - 1, banks[5], CHUNKS - 3)
                h_to_lo(l, UPS - 1, 1)
                dve.wait_ge(rstd_done, l * STATS + ST_M + 1)
                for n in range(2):
                    if n == 0:
                        dve.wait_ge(acc_mlp_half, l + 1)
                    else:
                        dve.wait_ge(weights_used, used(l, UNITS - 1))
                    for t in range(TOK):
                        add_to_x(acc_d[t][n], t, n, ST_M, x_updated)
            dve.wait_ge(final_gain_loaded, 16)
            dve.wait_ge(x_updated, 2 * TOK * (DEPTH + 1))
            for n in range(2):
                cols = slice(n * BANK, (n + 1) * BANK)
                dve.tensor_tensor((rope_a, rope_b)[n][:, :, :], x[:, :, cols],
                                         final_gain[:, cols].unsqueeze(1).broadcast_to([P, TOK, BANK]),
                                         ALU.mult).then_inc(x_gained, 1)
                if n == 0:
                    dve.wait_ge(summed, DEPTH * STATS + 3)
                    dve.scalar_tensor_tensor(out=means[:, ST_X, :], in0=sums[:, 0, :], scalar=NORM_EPS,
                                             in1=sums[:, 1, :], op0=ALU.add, op1=ALU.add).then_inc(mean_done, 1)
            t = 0
            dve.wait_ge(rstd_done, DEPTH * STATS + 1)
            dve.wait_ge(x_gained, 2)
            for n in range(2):
                dve.tensor_scalar(x[:, t, n * BANK:(n + 1) * BANK], (rope_a, rope_b)[n][:, t, :],
                                  rstd[:, ST_X, t:t + 1], None, ALU.mult).then_inc(final_0, 1)

        @block.tensor
        def _(pe):
            pe.sem_inc(weights_used, UNITS_HELD)
            pe.sem_inc(qk_turned, 4)
            pe.sem_inc(p_turned, 2)
            pe.sem_inc(pv_done, 2)
            pe.wait_ge(gains_loaded, 32)
            pe.transpose(banks[0][:, 0:n_gains], gain_rows[:, :], ident[0:n_gains, 0:n_gains])\
                .then_inc(gains_turned, 1)
            pe.wait_ge(gains_kept, 1)
            pe.wait_ge(x_loaded, 16 * TOK)

            def unit_ready(l, c, half):
                pe.wait_ge(split_done, l * UNITS + c * 2 + (half + 1 + UNITS_HELD))

            def three(out, s_hi, s_lo, m_hi, m_lo, first, last):
                pe.matmul(out, s_hi, m_hi, start=first, stop=False)
                pe.matmul(out, s_hi, m_lo, start=False, stop=False)
                return pe.matmul(out, s_lo, m_hi, start=False, stop=last)

            def turn(l, n, bank, src, k0):
                for k in range(2):
                    for t in range(TOK):
                        last = pe.transpose(bank[:, k * SEQ + t * P:k * SEQ + (t + 1) * P],
                                            src[:, t, (k0 + k) * P:(k0 + k + 1) * P], ident[:, :])
                last.then_inc(turned, 1)

            def project_in(l, s):
                u = s // 2
                g, k = u // 4, u % 4 * 2 + s % 2
                c = u // 2
                cols = slice((k % 4) * BANK, (k % 4 + 1) * BANK)
                if s % 2 == 0:
                    unit_ready(l, c, u % 2)
                if g == 0 and k % 2 == 0:
                    pe.wait_ge(turned_lo, l * TRS + TR_X + k // 2 + 1)
                if k == 0 and g in (2, 3, 5):
                    pe.wait_ge(rope_terms, l * 8 + 2 * ROPE_GROUPS[g - 2] + 2)
                if k == 0 and g == 4:
                    pe.wait_ge(v_done, l * 2 + 1)
                for t in range(TOK):
                    tok = slice(t * P, (t + 1) * P)
                    last = three(banks[2 * (g % 2) + t][:, :], xt_hi[:, k, tok], xt_lo[:, k, tok],
                                 w_hi[:, c % RING, cols], w_lo[:, c % RING, cols], k == 0, k == KT - 1)
                    if t == TOK - 1 and s % 2 == 1:
                        last.then_inc(weights_used, 1)

            def project_out(l, acc, k, u, t, n, first, last):
                c = u // 2
                cols = slice((u % 2) * UNIT + n * BANK, (u % 2) * UNIT + (n + 1) * BANK)
                tok = slice(t * P, (t + 1) * P)
                return three(acc[t][n][:, :], ot_hi[:, k, tok], ot_lo[:, k, tok],
                             w_hi[:, c % RING, cols], w_lo[:, c % RING, cols], first, last)

            def attention(l, s):
                if s in QKT_AT:
                    n = QKT_AT[s]
                    j = n // 2
                    pe.wait_ge(rope_done, l * 8 + 2 * j + 2)
                    pe.wait_ge(qk_copied, l * 8 + n + 1)
                    pe.wait_ge(p_copied, l * N_HEADS + sum(x_ < s for x_ in PT_AT) + 1)
                    for k in range(2):
                        for t in range(TOK):
                            f = 2 * (n % 2) + k
                            last = pe.transpose(t_bank[:, k * SEQ + t * P:k * SEQ + (t + 1) * P],
                                                roped[:, j % 2, t, f * P:(f + 1) * P], ident[:, :])
                    last.then_inc(qk_turned, 1)
                if s in PT_AT:
                    h = PT_AT[s]
                    pe.wait_ge(exp_done, l * N_HEADS + h + 3)
                    pe.wait_ge(p_copied, l * N_HEADS + h + 1)
                    pe.wait_ge(qk_copied, l * 8 + sum(x_ <= s for x_ in QKT_AT) + 1)
                    for n in range(3):
                        last = pe.transpose(t_bank[:, n * P:(n + 1) * P], probs[:, h % 2, n * P:(n + 1) * P],
                                            ident[:, :])
                    last.then_inc(p_turned, 1)
                if s in PV_AT:
                    h = PV_AT[s]
                    st, hh = h // SET_HEADS, h % SET_HEADS
                    pe.wait_ge(p_copied, l * N_HEADS + h + 2)
                    pe.wait_ge(v_done, l * 2 + st + 1)
                    if h % 4 == 0 and h > 0:
                        pe.wait_ge(o_done, l * 4 + h // 4)
                    cols = slice(hh * HEAD_DIM, (hh + 1) * HEAD_DIM)
                    pt = probs_t[:, h % 2, :]
                    o0 = o_bank[:, h % 4 * HEAD_DIM:(h % 4 + 1) * HEAD_DIM]
                    o1 = o_bank[:, (4 + h % 4) * HEAD_DIM:(5 + h % 4) * HEAD_DIM]
                    pe.matmul(o0, pt[:, 0:P], v[:, st, 0, cols], start=True, stop=True)
                    pe.matmul(o1, pt[:, P:2 * P], v[:, st, 0, cols], start=True, stop=False)
                    pe.matmul(o1, pt[:, 2 * P:3 * P], v[:, st, 1, cols], start=False, stop=True)\
                        .then_inc(pv_done, 1)
                if s in QK_AT:
                    h = QK_AT[s]
                    hh = h % SET_HEADS
                    rows = slice(hh % 2 * HEAD_DIM, (hh % 2 + 1) * HEAD_DIM)
                    if hh == 0:
                        pe.wait_ge(qk_copied, l * 8 + 4 * (h // SET_HEADS) + 5)
                    if h == SET_HEADS:
                        pe.wait_ge(turned_lo, l * TRS + TR_D + 2)
                    if hh >= 2:
                        pe.wait_ge(masked, l * N_HEADS + h - 1)
                    bank = s_banks[h % 2]
                    pe.matmul(bank[:, 0:P], q_t[rows, hh // 2, 0:P], k_t[rows, hh // 2, 0:P],
                              start=True, stop=True)
                    pe.matmul(bank[:, P:3 * P], q_t[rows, hh // 2, P:2 * P], k_t[rows, hh // 2, :],
                              start=True, stop=True).then_inc(scored, 1)
                if s == TURN_D:
                    pe.wait_ge(o_done, l * 4 + 2)
                    pe.wait_ge(masked, l * N_HEADS + SET_HEADS)
                    for n in range(2):
                        turn(l, TR_D + n, s_banks[n], o, 2 * n)
                if s == TURN_A:
                    pe.wait_ge(o_done, l * 4 + 3)
                    pe.wait_ge(masked, l * N_HEADS + N_HEADS)
                    turn(l, TR_A, s_banks[0], o, 0)

            def up(l, i, c, slot, bank):
                for f in range(2):
                    for k in range(KT):
                        if f == 0 and k % 4 == 0:
                            unit_ready(l, c, k // 4)
                        if i is None and f == 0 and k % 2 == 0:
                            pe.wait_ge(turned_lo, l * TRS + TR_M + k // 2 + 1)
                        cols = slice(k * SEQ + f * P, k * SEQ + (f + 1) * P)
                        last = three(bank[:, f * SEQ:(f + 1) * SEQ], w_hi[:, slot, cols], w_lo[:, slot, cols],
                                     xt_hi[:, k, :], xt_lo[:, k, :], k == 0, k == KT - 1)
                        if f == 1 and k % 4 == 3:
                            last.then_inc(weights_used, 1)

            def down(l, i, c, slot, b, first=False, last=False):
                pe.wait_ge(h_split, l * UPS + i + 1)
                if last:
                    unit_ready(l, c, 1)
                    for n in range(2):
                        for j in range(2):
                            for t in range(TOK):
                                cols = slice(j * UNIT + n * BANK, j * UNIT + (n + 1) * BANK)
                                tok = slice(t * P, (t + 1) * P)
                                mm = three(acc_d[t][n][:, :], h_hi[:, b, j, tok], h_lo[:, b, j, tok],
                                           w_hi[:, slot, cols], w_lo[:, slot, cols], False, j == 1)
                            if n == 1:
                                mm.then_inc(weights_used, 1)
                        if n == 0:
                            mm.then_inc(acc_mlp_half, 1)
                    return
                for j in range(2):
                    unit_ready(l, c, j)
                    for t in range(TOK):
                        for n in range(2):
                            cols = slice(j * UNIT + n * BANK, j * UNIT + (n + 1) * BANK)
                            tok = slice(t * P, (t + 1) * P)
                            mm = three(acc_d[t][n][:, :], h_hi[:, b, j, tok], h_lo[:, b, j, tok],
                                       w_hi[:, slot, cols], w_lo[:, slot, cols], first and j == 0, False)
                    mm.then_inc(weights_used, 1)

            with pe.Fori(0, DEPTH) as l:
                for n in range(4):
                    if n % 2 == 0:
                        pe.wait_ge(x_updated, l * 4 + n + 2)
                    turn(l, TR_X + n, banks[4 + n], x, 2 * n)
                for s in range(4 * IN_CHUNKS):
                    project_in(l, s)
                    attention(l, s)
                pe.wait_ge(rope_terms, l * 8 + 8)
                for u in range(2 * IN_CHUNKS, 2 * IN_CHUNKS + 4, 2):
                    k0 = u - 2 * IN_CHUNKS
                    for t in range(TOK):
                        for k in range(k0, k0 + 2):
                            if t == 0:
                                unit_ready(l, u // 2, k - k0)
                                if k % 2 == 0:
                                    pe.wait_ge(turned_lo, l * TRS + TR_D + k // 2 + 1)
                            elif k == 0:
                                pe.wait_ge(v_done, l * 2 + 2)
                            for n in range(2):
                                mm = project_out(l, acc_d, k, u + k - k0, t, n, k == 0, k == 3)
                            if t == TOK - 1:
                                mm.then_inc(weights_used, 1)
                            attention(l, 2 * u + 2 * t + k - k0)
                attention(l, TAIL)
                u0 = 2 * IN_CHUNKS + 4
                unit_ready(l, u0 // 2, 1)
                pe.wait_ge(turned_lo, l * TRS + TR_A + 1)
                pe.wait_ge(p_copied, l * N_HEADS + N_HEADS + 1)
                for n in range(2):
                    for k in range(2):
                        project_out(l, acc_a, 4 + k, u0 + k, 0, n, k == 0, False)
                pe.wait_ge(o_done, l * 4 + 4)
                turn(l, TR_A + 1, s_banks[1], o, 2)
                for n in (1, 0):
                    if n == 0:
                        pe.wait_ge(turned_lo, l * TRS + TR_A + 2)
                    for k in range(2):
                        mm = project_out(l, acc_a, 4 + k, u0 + k, 1, n, k == 0, False)
                        if n == 0:
                            mm.then_inc(weights_used, 1)
                unit_ready(l, u0 // 2 + 1, 1)
                for n in range(2):
                    for k in range(2, 4):
                        for t in range(TOK):
                            mm = project_out(l, acc_a, 4 + k, u0 + k, t, n, False, k == 3)
                        if n == 1:
                            mm.then_inc(weights_used, 1)
                    if n == 0:
                        mm.then_inc(acc_a_half, 1)
                for n in range(4):
                    if n % 2 == 0:
                        pe.wait_ge(x_mid, l * 4 + n + 2)
                    turn(l, TR_M + n, banks[n], x, 2 * n)
                up(l, None, FIRST_UP, FIRST_UP % RING, banks[4])
                up(l, 1, FIRST_UP + 1, 1, banks[5])
                down(l, 0, FIRST_UP + 2, 2, 0, first=True)
                with pe.Fori(0, MLP_TURNS) as j:
                    c = j * 4 + (FIRST_UP + 3)
                    up(l, 0, c, 3, banks[4])
                    down(l, j * 2 + 1, c + 1, 0, 1)
                    up(l, 0, c + 2, 1, banks[5])
                    down(l, j * 2 + 2, c + 3, 2, 0)
                down(l, UPS - 1, CHUNKS - 1, (CHUNKS - 1) % RING, 1, last=True)


def shape_constants():
    ident = np.eye(P, dtype=np.float32)
    inv = (1.0 / ROPE_THETA ** (np.arange(0, HEAD_DIM, 2, dtype=np.float64) / HEAD_DIM)).astype(np.float32)
    ang = (np.arange(SEQ, dtype=np.float32)[:, None] * inv[None, :]).astype(np.float64)
    rope = np.concatenate([np.cos(ang), np.sin(ang), -np.sin(ang)], axis=1).astype(np.float32)
    rope = np.ascontiguousarray(rope.reshape(TOK, P, 3 * HALF).transpose(1, 0, 2))
    d = np.arange(P)[:, None] - np.arange(2 * P)[None, :] + P
    counts = sum(((d <= w) & (d % r == 0)).astype(np.int64) for w, r in DILATED_CONFIGS)
    dilated = np.where((d >= 0) & (counts > 0), np.log(np.maximum(counts, 1)) / SCALE, NEG_INF)
    causal = np.where(d >= 0, 0.0, NEG_INF)
    masks = np.ascontiguousarray(np.stack([dilated, causal], axis=1).astype(np.float32))
    return ident, masks, rope


_INS = ["x", "w_in", "w_out", "w_up", "w_down", "final_norm"]


def kernel(**inputs):
    import numpy as _np
    import concourse.bacc as _bacc
    from concourse import mybir as _mybir
    from concourse.bass_utils import run_bass_kernel_spmd as _run

    nc = _bacc.Bacc("TRN2", target_bir_lowering=False, num_devices=1)
    arrays = {f"in_{name}": _np.ascontiguousarray(inputs[name]) for name in _INS}
    arrays["in_gain_rows"] = _np.concatenate(
        [_np.asarray(inputs[name]).reshape(-1, P)
         for name in ("attn_norm", "mlp_norm", "moba_out_norm", "dil_out_norm")])
    arrays |= dict(zip(("c_ident", "c_masks", "c_rope"), shape_constants()))
    args = [nc.dram_tensor(n, a.shape, _mybir.dt.from_np(a.dtype), kind="ExternalInput").ap()
            for n, a in arrays.items()]
    args.append(nc.dram_tensor("out", (1, SEQ, D_MODEL), _mybir.dt.float32, kind="ExternalOutput").ap())
    hybrid_kernel(nc, *args)
    r = _run(nc, [arrays], core_ids=[0])
    return r.results[0]["out"]
```

```python
import numpy as np

import concourse.bass as bass
from concourse import mybir
from contextlib import ExitStack

F32 = mybir.dt.float32
F32R = mybir.dt.float32r
BF16 = mybir.dt.bfloat16
ALU = mybir.AluOpType
ACT = mybir.ActivationFunctionType

P = 128
D_MODEL = 1024
SEQ = 256
DEPTH = 2
HEAD_DIM = 64
HALF = HEAD_DIM // 2
N_HEADS = D_MODEL // HEAD_DIM
SET_HEADS = N_HEADS // 2
D_SET = SET_HEADS * HEAD_DIM
D_FF = 4 * D_MODEL
SCALE = HEAD_DIM ** -0.5
DILATED_CONFIGS = ((128, 1), (512, 4), (2048, 16))
ROPE_THETA = 10000.0
NORM_EPS = 1e-6
NEG_INF = -1e30

TOK = SEQ // P
KT = D_MODEL // P
BANK = 512

CHUNK = 2048
UNIT = CHUNK // 2
RING = 4
UNITS_HELD = 2 * RING
GROUPS = 3 * D_MODEL // BANK
IN_CHUNKS = 2 * GROUPS
OUT_CHUNKS = D_MODEL * D_MODEL // (P * CHUNK)
ATT_UNITS = 2 * (IN_CHUNKS + OUT_CHUNKS)
UPS = D_FF // BANK * 2
CHUNKS = IN_CHUNKS + OUT_CHUNKS + 2 * UPS
UNITS = 2 * CHUNKS
FIRST_UP = IN_CHUNKS + OUT_CHUNKS
WARM_UP = (8, 4)
HI_AHEAD = 6
LO_AHEAD = 4
VISITS = CHUNKS // RING
MLP_TURNS = (UPS - 2) // 2
SPLIT_TURNS = MLP_TURNS - 1

GROUP_COLUMNS = [3, 4, 5, 0, 1, 2]
ROPE_GROUPS = {0: 0, 1: 1, 3: 2, 4: 3}
V_GROUPS = {2: 0, 5: 1}

QK_AT = {23 + 2 * h if h < 8 else 38 + h: h for h in range(N_HEADS)}
PT_AT = {s + 2: h for s, h in QK_AT.items()}
PV_AT = {s + 3: h for s, h in QK_AT.items()}
QKT_AT = {12: 0, 13: 1, 20: 2, 21: 3, 38: 4, 40: 5, 44: 6, 47: 7}
ROPE_AT = {8 * g + 8: g for g in ROPE_GROUPS}
V_AT = {8 * g + 8: g for g in V_GROUPS}
TAIL = 56
O_AT = {s: h // 4 for s, h in PV_AT.items() if h % 4 == 3}
TURN_D, TURN_A = 42, 54
X_AT = {58 + n: n for n in range(2 * TOK)}

TR_X, TR_D, TR_A, TR_M, TRS = 0, 8, 12, 16, 24
ST_X, ST_D, ST_A, ST_M, STATS = 0, 1, 2, 3, 4


def hybrid_kernel(nc, x_d, w_in, w_out, w_up, w_down, final_g, gain_rows_d, ident_d, masks_d, rope_d,
                  out_d):
    ctx = ExitStack()
    with ctx:
        def sb(name, shape, dt=F32):
            return ctx.enter_context(nc.sbuf_tensor(name, [P, *shape], dt))

        def sem(name):
            return ctx.enter_context(nc.semaphore(name))

        raw = sb("raw", [RING, CHUNK])
        w_hi = sb("w_hi", [RING, CHUNK], F32R)
        w_lo = sb("w_lo", [RING, CHUNK], F32R)
        x = sb("x", [TOK, D_MODEL])
        xt_hi = sb("xt_hi", [KT, SEQ], F32R)
        xt_lo = sb("xt_lo", [KT, SEQ], F32R)
        ot_hi = sb("ot_hi", [KT, SEQ], F32R)
        ot_lo = sb("ot_lo", [KT, SEQ], F32R)
        squares = sb("squares", [TOK, D_MODEL], BF16)
        rope_a = sb("rope_a", [TOK, D_SET])
        rope_b = sb("rope_b", [TOK, D_SET])
        roped = sb("roped", [2, TOK, D_SET])
        v = sb("v", [2, TOK, D_SET])
        q_t = sb("q_t", [4, SEQ])
        k_t = sb("k_t", [4, SEQ])
        scores = sb("scores", [2, 3 * P])
        probs = sb("probs", [2, 3 * P])
        probs_t = sb("probs_t", [2, 3 * P])
        row_max = sb("row_max", [2, TOK])
        row_bias = sb("row_bias", [2, TOK])
        row_sum = sb("row_sum", [TOK, N_HEADS])
        row_inv = sb("row_inv", [TOK, N_HEADS])
        o = sb("o", [TOK, D_SET])
        up_relu = sb("up_relu", [2 * SEQ])
        up_sq = sb("up_sq", [2 * SEQ])
        h_hi = sb("h_hi", [2, 2, SEQ], F32R)
        h_lo = sb("h_lo", [2, 2, SEQ], F32R)
        masks = sb("masks", [2, 2 * P])
        ident = sb("ident", [P])
        rope_tab = sb("rope_tab", [TOK, 3 * HALF])
        rope_r = sb("rope_r", [TOK, 3 * HALF])
        layer_gains = 2 * KT + 2 * 4
        n_gains = DEPTH * layer_gains
        gain_rows = ctx.enter_context(nc.sbuf_tensor("gain_rows", [n_gains, P], F32))
        gains_all = sb("gains_all", [n_gains + layer_gains])
        gains = sb("gains", [layer_gains])
        final_gain = sb("final_gain", [D_MODEL])
        sums = sb("sums", [STATS, TOK])
        means = sb("means", [STATS, TOK])
        rstd = sb("rstd", [STATS, TOK])
        powers = sb("powers", [2, TOK])

        banks = [ctx.enter_context(nc.psum_tensor(f"bank{n}", [P, BANK], F32)) for n in range(8)]
        s_banks, t_bank, o_bank = banks[4:6], banks[6], banks[7]
        acc_d = [[banks[2 * t + n] for n in range(2)] for t in range(TOK)]
        acc_a = [[banks[4], banks[6]], [banks[5], banks[7]]]
        x_banks, m_banks = banks[4:8], banks[0:4]
        up_0 = [banks[4], banks[6]]

        x_loaded = [sem(f"x_loaded{n}") for n in range(2)]
        masks_loaded = sem("masks_loaded")
        gains_loaded = sem("gains_loaded")
        rope_loaded = sem("rope_loaded")
        final_gain_loaded = sem("final_gain_loaded")
        powers_set = sem("powers_set")
        zeros_set = sem("zeros_set")
        gains_turned = sem("gains_turned")
        gains_kept = sem("gains_kept")
        raw_ready = [sem(f"raw_ready{n}") for n in range(RING)]
        first_lo_half = sem("first_lo_half")
        first_ready = sem("first_ready")
        hi_done = sem("hi_done")
        split_done = sem("split_done")
        weights_used = sem("weights_used")
        x_updated = sem("x_updated")
        x_mid = sem("x_mid")
        x_d_added = sem("x_d_added")
        turned = sem("turned")
        turned_hi = sem("turned_hi")
        turned_lo = sem("turned_lo")
        summed = sem("summed")
        mean_done = sem("mean_done")
        rstd_done = sem("rstd_done")
        rope_scaled = sem("rope_scaled")
        gains_done = sem("gains_done")
        rope_terms = sem("rope_terms")
        rope_done = sem("rope_done")
        v_done = sem("v_done")
        qk_turned = sem("qk_turned")
        qk_copied = sem("qk_copied")
        scored = sem("scored")
        masked = sem("masked")
        bias_done = sem("bias_done")
        exp_done = sem("exp_done")
        p_turned = sem("p_turned")
        p_copied = sem("p_copied")
        pv_done = sem("pv_done")
        inv_done = sem("inv_done")
        o_done = sem("o_done")
        acc_a_done = sem("acc_a_done")
        acc_mlp_done = sem("acc_mlp_done")
        relu_done = sem("relu_done")
        h_done = sem("h_done")
        h_hi_done = sem("h_hi_done")
        h_split = sem("h_split")
        x_gained = sem("x_gained")
        final_0 = sem("final_0")
        final_1 = sem("final_1")
        out_written = sem("out_written")

        block = ctx.enter_context(nc.Block())

        x_v = x_d[0].rearrange("(t p) n -> p t n", p=P)
        in_v = w_in.rearrange("l (k p) n -> l p k n", p=P)
        out_v = w_out.rearrange("l (k p) n -> l p k n", p=P)
        up_v = w_up.rearrange("l (k p) n -> l p k n", p=P)
        down_v = w_down.rearrange("l (k p) n -> l p k n", p=P)

        def used(l, u):
            return l * UNITS + u + (1 + UNITS_HELD)

        def turned_tile(x_or_m, k):
            return x_or_m[k % 4][:, k // 4 * SEQ:(k // 4 + 1) * SEQ]

        def pair(bank, n):
            return bank[:, n % 2 * SEQ:(n % 2 + 1) * SEQ]

        def visit(l, c):
            return l * (16 * VISITS) + 16 * (c // RING + 1)

        def wait_all(eng, constant, *others):
            values = [eng.compute_val(value) for _, value in others]
            eng.wait_ge(*constant)
            for (other, _), value in zip(others, values):
                eng.wait_ge(other, value)

        @block.sync
        def _(sp):
            sp.dma_start(x[:, :, 0:BANK], x_v[:, :, 0:BANK]).then_inc(x_loaded[0], 16)
            sp.dma_start(ident[:, :], ident_d).then_inc(gains_loaded, 16)

            def load(l, c, slot, src, k, after_first=False):
                pool_too = [(first_lo_half, l + 1)] if after_first else []
                wait_all(sp, (split_done, UNITS_HELD), (split_done, l * UNITS + c * 2 + 2), *pool_too)
                sp.dma_start(raw[:, slot, :].rearrange("p (k n) -> p k n", k=k), src)\
                    .then_inc(raw_ready[slot], 16)

            def at(view, l):
                return view[bass.ds(l, 1)].rearrange("a p k n -> p (a k) n")

            with sp.Fori(0, DEPTH) as l:
                cols = GROUP_COLUMNS[0] * BANK
                wait_all(sp, (split_done, UNITS_HELD), (split_done, l * UNITS + 2))
                for half, ready in enumerate((first_ready, raw_ready[0])):
                    sp.dma_start(raw[:, 0, half * UNIT:(half + 1) * UNIT].rearrange("p (k n) -> p k n", k=2),
                                 at(in_v[:, :, 2 * half:2 * half + 2, cols:cols + BANK], l))\
                        .then_inc(ready, 16)
                for c in range(1, IN_CHUNKS):
                    cols = GROUP_COLUMNS[c // 2] * BANK
                    load(l, c, c % RING, at(in_v[:, :, 4 * (c % 2):4 * (c % 2) + 4, cols:cols + BANK], l), 4,
                         after_first=c == RING)
                for n in range(OUT_CHUNKS):
                    c = IN_CHUNKS + n
                    k = 2 * ((n + 2) % OUT_CHUNKS)
                    load(l, c, c % RING, at(out_v[:, :, k:k + 2, :], l), 2)

                def load_up(l, c, i, slot):
                    src = up_v[bass.ds(l, 1), :, :, bass.ds(i * SEQ, SEQ)]
                    load(l, c, slot, src.rearrange("a p k n -> p (a k) n"), KT)

                def load_down(l, c, i, slot):
                    src = down_v[bass.ds(l, 1), :, bass.ds(i * 2, 2), :]
                    load(l, c, slot, src.rearrange("a p k n -> p (a k) n"), 2)

                load_up(l, FIRST_UP, 0, FIRST_UP % RING)
                with sp.Fori(0, MLP_TURNS) as j:
                    c = j * 4 + (FIRST_UP + 1)
                    load_up(l, c, j * 2 + 1, 1)
                    load_down(l, c + 1, j * 2, 2)
                    load_up(l, c + 2, j * 2 + 2, 3)
                    load_down(l, c + 3, j * 2 + 1, 0)
                load_up(l, CHUNKS - 3, UPS - 1, 1)
                load_down(l, CHUNKS - 2, UPS - 2, 2)
                load_down(l, CHUNKS - 1, UPS - 1, 3)

            sp.dma_start(final_gain[:, :], final_g.rearrange("(a n) -> a n", a=1).broadcast_to([P, D_MODEL]))\
                .then_inc(final_gain_loaded, 16)
            for n in range(2):
                cols = slice(n * BANK, (n + 1) * BANK)
                sp.wait_ge(final_0, n + 1)
                sp.dma_start(out_d[0][0:P, cols], x[:, 0, cols]).then_inc(out_written, 16)
            sp.wait_ge(out_written, 16 * 4)

        @block.gpsimd
        def _(pool):
            pool.memset(powers[:, 0, :], -0.5).then_inc(powers_set, 1)
            pool.memset(powers[:, 1, :], -1.0).then_inc(powers_set, 1)

            def inverse_rms(l, n, width):
                wait_all(pool, (powers_set, 2), (summed, l * STATS + n + 2))
                pool.tensor_scalar(means[:, n, :], sums[:, n, :], 1.0 / width, NORM_EPS,
                                   ALU.mult, ALU.add).then_inc(mean_done, 1)
                pool.wait_ge(mean_done, l * STATS + n + 1)
                pool.tensor_tensor(rstd[:, n, :], means[:, n, :], powers[:, int(n == ST_M), :],
                                   ALU.pow).then_inc(rstd_done, 1)

            def rope_sum(l, j, t):
                pool.wait_ge(rope_terms, l * 8 + 2 * j + t + 1)
                if t == 0:
                    pool.wait_ge(qk_turned, l * 8 + 2 * j + 2)
                pool.tensor_tensor(roped[:, j % 2, t, :], rope_a[:, t, :], rope_b[:, t, :], ALU.add)\
                    .then_inc(rope_done, 1)

            with pool.Fori(0, DEPTH) as l:
                pool.wait_ge(hi_done, l * UNITS + 1)
                pool.tensor_tensor(w_lo[:, 0, 0:BANK], raw[:, 0, 0:BANK], w_hi[:, 0, 0:BANK].bitcast(F32),
                                   ALU.subtract).then_inc(first_lo_half, 1)
                inverse_rms(l, ST_X, D_MODEL)
                wait_all(pool, (rope_loaded, 16), (rstd_done, l * STATS + ST_X + 1))
                for t in range(TOK):
                    last = pool.tensor_scalar(rope_r[:, t, :], rope_tab[:, t, :],
                                              rstd[:, ST_X, t:t + 1], None, ALU.mult)
                last.then_inc(rope_scaled, 1)
                for j in range(4):
                    for t in range(TOK):
                        rope_sum(l, j, t)
                inverse_rms(l, ST_D, D_SET)
                inverse_rms(l, ST_A, D_SET)
                inverse_rms(l, ST_M, D_MODEL)
            for t in range(TOK):
                pool.wait_ge(mean_done, DEPTH * STATS + t + 1)
                pool.tensor_tensor(rstd[:, ST_X, t:t + 1], means[:, ST_X, t:t + 1], powers[:, 0, t:t + 1],
                                   ALU.pow).then_inc(rstd_done, 1)

        @block.scalar
        def _(act):
            act.dma_start(gain_rows[:, :], gain_rows_d).then_inc(gains_loaded, 16)
            act.wait_ge(powers_set, 2)
            act.activation(squares[:, 0, 0:TOK], powers[:, 0, :], ACT.Copy).then_inc(summed, 1)
            act.wait_ge(summed, 1)
            act.dma_start(x[:, :, BANK:2 * BANK], x_v[:, :, BANK:2 * BANK]).then_inc(x_loaded[1], 16)
            act.dma_start(rope_tab[:, :, :], rope_d).then_inc(rope_loaded, 16)
            act.dma_start(masks[:, :, :], masks_d).then_inc(masks_loaded, 16)
            act.sem_inc(qk_copied, 1)
            act.sem_inc(p_copied, 1)
            act.sem_inc(exp_done, 2)

            def hi(l, c, slot, half, seen=None):
                if seen is not None:
                    act.wait_ge(raw_ready[slot], seen)
                act.wait_ge(weights_used, l * UNITS + c * 2 + (half + 1))
                part = slice(half * UNIT, (half + 1) * UNIT)
                act.copy(w_hi[:, slot, part], raw[:, slot, part]).then_inc(hi_done, 1)

            def turned_to_hi(l, n, tile, dst, gain):
                act.wait_ge(turned, l * TRS + n + 1)
                if n == TR_X:
                    act.wait_ge(gains_done, l + 1)
                act.activation(dst, tile, ACT.Copy, scale=gains[:, gain:gain + 1]).then_inc(turned_hi, 1)

            def pair_to_hi(l, tr, k, bank, k0, gain0):
                for n in (k, k + 1):
                    turned_to_hi(l, tr + n, pair(bank, n), ot_hi[:, k0 + n, :], gain0 + n)

            def square_sums(l, n, src, width):
                act.wait_ge(summed, l * STATS + n + 1)
                for t in range(TOK):
                    last = act.activation(squares[:, t, 0:width], src[:, t, :], ACT.Square,
                                          accum_out=sums[:, n, t:t + 1])
                last.then_inc(summed, 1)

            with act.Fori(0, DEPTH) as l:
                for u in range(HI_AHEAD):
                    if u == 0:
                        act.wait_ge(first_ready, l * 16 + 16)
                    hi(l, u // 2, u // 2 % RING, u % 2, visit(l, u // 2) if u > 0 else None)
                    if u in (0, 2):
                        for k in range(2 * u, 2 * u + 4):
                            turned_to_hi(l, TR_X + k, turned_tile(x_banks, k), xt_hi[:, k, :], k)
                square_sums(l, ST_X, x, D_MODEL)
                for s in range(2 * ATT_UNITS):
                    u = s // 2 + HI_AHEAD
                    if s in V_AT:
                        g = V_AT[s]
                        act.wait_ge(weights_used, used(l, 4 * g + 3))
                        act.wait_ge(rstd_done, l * STATS + ST_X + 1)
                        for t in range(TOK):
                            last = act.activation(v[:, V_GROUPS[g], t, :], banks[2 * (g % 2) + t][:, :],
                                                  ACT.Copy, scale=rstd[:, ST_X, t:t + 1])
                        last.then_inc(v_done, 1)
                    if s in QKT_AT:
                        n = QKT_AT[s]
                        dst = (q_t, k_t)[n // 2 % 2]
                        act.wait_ge(qk_turned, l * 8 + n + 5)
                        act.copy(dst[:, 2 * (n % 2):2 * (n % 2) + 2, :],
                                 t_bank[:, :].rearrange("p (a b) -> p a b", a=2)).then_inc(qk_copied, 1)
                    if s in PT_AT:
                        h = PT_AT[s]
                        act.wait_ge(p_turned, l * N_HEADS + h + 3)
                        act.wait_ge(pv_done, l * N_HEADS + h + 1)
                        act.copy(probs_t[:, h % 2, :], t_bank[:, 0:3 * P]).then_inc(p_copied, 1)
                    if s in QK_AT:
                        h = QK_AT[s]
                        act.wait_ge(bias_done, l * N_HEADS + h + 1)
                        act.wait_ge(p_turned, l * N_HEADS + h + 1)
                        for t in range(TOK):
                            cols = slice(0, P) if t == 0 else slice(P, 3 * P)
                            last = act.activation(probs[:, h % 2, cols], scores[:, h % 2, cols], ACT.Exp,
                                                  scale=SCALE, bias=row_bias[:, h % 2, t:t + 1],
                                                  accum_out=row_sum[:, t, h:h + 1])
                        last.then_inc(exp_done, 1)
                    if s == TURN_D:
                        for n in range(2):
                            pair_to_hi(l, TR_D, 2 * n, s_banks[n], 0, 2 * KT + 4)
                        square_sums(l, ST_D, o, D_SET)
                    if s == TURN_A:
                        pair_to_hi(l, TR_A, 0, s_banks[0], 4, 2 * KT)
                    if s == TAIL:
                        pair_to_hi(l, TR_A, 2, s_banks[1], 4, 2 * KT)
                        square_sums(l, ST_A, o, D_SET)
                    if s % 2 == 0 and u < 2 * (FIRST_UP + 2):
                        hi(l, u // 2, u // 2 % RING, u % 2, visit(l, u // 2))
                for k in range(KT):
                    turned_to_hi(l, TR_M + k, turned_tile(m_banks, k), xt_hi[:, k, :], KT + k)
                square_sums(l, ST_M, x, D_MODEL)

                def h_to_hi(l, i, b):
                    act.wait_ge(h_done, l * UPS + i + 1)
                    act.wait_ge(weights_used, used(l, i * 4 + (2 * (FIRST_UP - 2) + 1)))
                    act.copy(h_hi[:, b, :, :], up_sq[:, :].rearrange("p (a b) -> p a b", a=2))\
                        .then_inc(h_hi_done, 1)

                def hi_chunk(l, c, slot, seen):
                    for half in range(2):
                        hi(l, c, slot, half, seen if half == 0 else None)

                hi_chunk(l, FIRST_UP + 2, (FIRST_UP + 2) % RING, visit(l, FIRST_UP + 2))
                h_to_hi(l, 0, 0)
                for c in (FIRST_UP + 3, FIRST_UP + 4):
                    hi_chunk(l, c, c % RING, visit(l, c))
                with act.Fori(0, SPLIT_TURNS) as j:
                    for b in range(2):
                        h_to_hi(l, j * 2 + (1 + b), (1 + b) % 2)
                        for c in (FIRST_UP + 5 + 2 * b, FIRST_UP + 6 + 2 * b):
                            hi_chunk(l, j * 4 + c, c % RING, visit(l, c) + j * 16)
                h_to_hi(l, UPS - 3, 1)
                for c in (CHUNKS - 3, CHUNKS - 2):
                    hi_chunk(l, c, c % RING, visit(l, c))
                h_to_hi(l, UPS - 2, 0)
                hi_chunk(l, CHUNKS - 1, (CHUNKS - 1) % RING, visit(l, CHUNKS - 1))
                h_to_hi(l, UPS - 1, 1)
            for n in range(2):
                for t in range(TOK):
                    act.wait_ge(x_updated, 2 * TOK * DEPTH + 2 * n + t + 1)
                    act.wait_ge(summed, DEPTH * STATS + 2 * n + t + 1)
                    act.activation(squares[:, t, n * BANK:(n + 1) * BANK],
                                   x[:, t, n * BANK:(n + 1) * BANK], ACT.Square,
                                   scale=D_MODEL ** -0.5, accum_out=sums[:, n, t:t + 1]).then_inc(summed, 1)
            t = 1
            act.wait_ge(rstd_done, DEPTH * STATS + 2)
            for n in range(2):
                act.wait_ge(x_gained, n + 1)
                act.activation(x[:, t, n * BANK:(n + 1) * BANK], (rope_a, rope_b)[n][:, t, :], ACT.Copy,
                               scale=rstd[:, ST_X, t:t + 1]).then_inc(final_1, 1)
                act.wait_ge(final_1, n + 1)
                act.dma_start(out_d[0][t * P:(t + 1) * P, n * BANK:(n + 1) * BANK],
                              x[:, t, n * BANK:(n + 1) * BANK]).then_inc(out_written, 16)

        @block.vector
        def _(dve):
            dve.sem_inc(split_done, UNITS_HELD)
            dve.sem_inc(x_updated, 2 * TOK)

            def lo(l, c, slot, half, start=0):
                dve.wait_ge(hi_done, l * UNITS + c * 2 + (half + 1))
                part = slice(half * UNIT + start, (half + 1) * UNIT)
                dve.tensor_tensor(w_lo[:, slot, part], raw[:, slot, part],
                                  w_hi[:, slot, part].bitcast(F32), ALU.subtract).then_inc(split_done, 1)

            def turned_to_lo(l, n, tile, hi_t, lo_t, gain, left):
                dve.wait_ge(turned_hi, l * TRS + left + 1)
                dve.scalar_tensor_tensor(out=lo_t, in0=tile, scalar=gains[:, gain:gain + 1],
                                         in1=hi_t.bitcast(F32), op0=ALU.mult, op1=ALU.subtract)\
                    .then_inc(turned_lo, 1)

            def x_to_lo(l, tr, tiles, k, gain0):
                turned_to_lo(l, tr + k, turned_tile(tiles, k), xt_hi[:, k, :], xt_lo[:, k, :], gain0 + k, tr + k)

            def pair_to_lo(l, tr, k, bank, k0, gain0):
                for n in (k, k + 1):
                    turned_to_lo(l, tr + n, pair(bank, n), ot_hi[:, k0 + n, :], ot_lo[:, k0 + n, :], gain0 + n,
                                 tr + k + 1)

            def add_to_x(bank, t, n, stat, done):
                part = x[:, t, n * BANK:(n + 1) * BANK]
                dve.scalar_tensor_tensor(out=part, in0=bank[:, :], scalar=rstd[:, stat, t:t + 1], in1=part,
                                         op0=ALU.mult, op1=ALU.add).then_inc(done, 1)

            def rope_products(l, g, t):
                j = ROPE_GROUPS[g]
                dve.wait_ge(weights_used, used(l, 4 * g + 3))
                dve.wait_ge(rope_scaled, l + 1)
                if j > 0:
                    dve.wait_ge(rope_done, l * 8 + 2 * (j - 1) + t + 1)
                bank = banks[2 * (g % 2) + t]
                cos, sin, neg = (rope_r[:, t, n * HALF:(n + 1) * HALF] for n in range(3))

                def wide(table, n):
                    return table.unsqueeze(1).broadcast_to([P, n, HALF])

                halves = bank[:, :].rearrange("p (a c) -> p a c", c=HALF)
                dve.tensor_tensor(rope_a[:, t, :].rearrange("p (a c) -> p a c", c=HALF), halves,
                                  wide(cos, 2 * SET_HEADS), ALU.mult)
                b = rope_b[:, t, :].rearrange("p (a c) -> p a c", c=HALF)
                dve.tensor_tensor(b[:, 0::2, :], halves[:, 1::2, :], wide(neg, SET_HEADS), ALU.mult)
                dve.tensor_tensor(b[:, 1::2, :], halves[:, 0::2, :], wide(sin, SET_HEADS), ALU.mult)\
                    .then_inc(rope_terms, 1)

            dve.memset(probs[:, 0, 0:P], 0.0).then_inc(zeros_set, 1)
            dve.wait_ge(gains_turned, 1)
            dve.tensor_copy(gains[:, :], banks[0][:, 0:layer_gains]).then_inc(gains_done, 1)
            dve.tensor_copy(gains_all[:, 0:n_gains], banks[0][:, 0:n_gains])
            dve.tensor_copy(gains_all[:, n_gains:n_gains + layer_gains], banks[0][:, 0:layer_gains])\
                .then_inc(gains_kept, 1)

            with dve.Fori(0, DEPTH) as l:
                dve.wait_ge(gains_done, l + 1)
                x_to_lo(l, TR_X, x_banks, 0, 0)
                lo(l, 0, 0, 0, BANK)
                for k in range(1, 4):
                    x_to_lo(l, TR_X, x_banks, k, 0)
                lo(l, 0, 0, 1)
                lo(l, 1, 1, 0)
                for k in range(4, KT):
                    x_to_lo(l, TR_X, x_banks, k, 0)
                lo(l, 1, 1, 1)
                for s in range(2 * ATT_UNITS):
                    u = s // 2 + LO_AHEAD
                    if s in O_AT:
                        four = O_AT[s]
                        heads = slice(4 * four, 4 * four + 4)
                        dve.wait_ge(pv_done, l * N_HEADS + 4 * four + 4 + 2)
                        dve.reciprocal(row_inv[:, :, heads], row_sum[:, :, heads]).then_inc(inv_done, 1)
                        dve.wait_ge(inv_done, l * 4 + four + 1)
                        if four == 2:
                            dve.wait_ge(summed, l * STATS + ST_D + 2)
                        cols = four % 2 * 4 * HEAD_DIM
                        for t in range(TOK):
                            last = dve.tensor_tensor(
                                o[:, t, cols:cols + 4 * HEAD_DIM].rearrange("p (h d) -> p h d", h=4),
                                o_bank[:, t * 4 * HEAD_DIM:(t + 1) * 4 * HEAD_DIM].rearrange("p (h d) -> p h d", h=4),
                                row_inv[:, t, heads].unsqueeze(2).broadcast_to([P, 4, HEAD_DIM]), ALU.mult)
                        last.then_inc(o_done, 1)
                    if s in QK_AT:
                        h = QK_AT[s]
                        m = masks[:, h // SET_HEADS, :]
                        wait_all(dve, (masks_loaded, 16), (scored, l * N_HEADS + h + 1),
                                 (exp_done, l * N_HEADS + h + 1))
                        bank = s_banks[h % 2]
                        dve.tensor_tensor_reduce(out=scores[:, h % 2, 0:P], in0=bank[:, 0:P], in1=m[:, P:2 * P],
                                                 scale=1.0, scalar=-3.0e38, op0=ALU.add, op1=ALU.max,
                                                 accum_out=row_max[:, h % 2, 0:1])
                        dve.tensor_tensor_reduce(out=scores[:, h % 2, P:3 * P], in0=bank[:, P:3 * P], in1=m,
                                                 scale=1.0, scalar=-3.0e38, op0=ALU.add, op1=ALU.max,
                                                 accum_out=row_max[:, h % 2, 1:2]).then_inc(masked, 1)
                        dve.wait_ge(masked, l * N_HEADS + h + 1)
                        dve.tensor_scalar(row_bias[:, h % 2, :], row_max[:, h % 2, :], -SCALE, None, ALU.mult)\
                            .then_inc(bias_done, 1)
                    if s in ROPE_AT:
                        for t in range(TOK):
                            rope_products(l, ROPE_AT[s], t)
                    if s == TURN_D:
                        for n in range(2):
                            pair_to_lo(l, TR_D, 2 * n, s_banks[n], 0, 2 * KT + 4)
                    if s == TURN_A:
                        pair_to_lo(l, TR_A, 0, s_banks[0], 4, 2 * KT)
                    if s == TAIL:
                        pair_to_lo(l, TR_A, 2, s_banks[1], 4, 2 * KT)
                    if s in X_AT:
                        n, t = divmod(X_AT[s], TOK)
                        if X_AT[s] == 0:
                            dve.wait_ge(weights_used, used(l, 2 * IN_CHUNKS + 3))
                            dve.wait_ge(rstd_done, l * STATS + ST_D + 1)
                        add_to_x(acc_d[t][n], t, n, ST_D, x_d_added)
                    if s % 2 == 1 and u < 2 * FIRST_UP + 1:
                        lo(l, u // 2, u // 2 % RING, u % 2)
                dve.wait_ge(rstd_done, l * STATS + ST_A + 1)
                dve.wait_ge(x_d_added, l * 4 + 4)
                for n in range(2):
                    for t in range(TOK):
                        if (n, t) == (1, 1):
                            for k in range(3):
                                x_to_lo(l, TR_M, m_banks, k, KT)
                            dve.wait_ge(weights_used, used(l, ATT_UNITS - 1))
                        else:
                            dve.wait_ge(acc_a_done, l * 3 + 2 * n + t + 1)
                        add_to_x(acc_a[t][n], t, n, ST_A, x_mid)
                x_to_lo(l, TR_M, m_banks, 3, KT)
                lo(l, FIRST_UP, FIRST_UP % RING, 1)
                for k in range(4, KT):
                    x_to_lo(l, TR_M, m_banks, k, KT)
                dve.wait_ge(gains_kept, 1)
                dve.wait_ge(turned_lo, (l + 1) * TRS)
                dve.tensor_copy(gains[:, :], gains_all[:, bass.ds((l + 1) * layer_gains, layer_gains)])\
                    .then_inc(gains_done, 1)

                def square_relu(l, i, tiles, c):
                    dve.wait_ge(weights_used, used(l, c * 2 + 1))
                    at = 0
                    for tile in tiles:
                        last = dve.tensor_scalar(up_relu[:, at:at + tile.shape[1]], tile, 0.0, None, ALU.max)
                        at += tile.shape[1]
                    last.then_inc(relu_done, 1)
                    dve.wait_ge(relu_done, l * UPS + i + 1)
                    dve.tensor_tensor(up_sq[:, :], up_relu[:, :], up_relu[:, :], ALU.mult).then_inc(h_done, 1)

                def h_to_lo(l, i, b):
                    dve.wait_ge(h_hi_done, l * UPS + i + 1)
                    dve.tensor_tensor(h_lo[:, b, :, :], up_sq[:, :].rearrange("p (a b) -> p a b", a=2),
                                      h_hi[:, b, :, :].bitcast(F32), ALU.subtract).then_inc(h_split, 1)

                def lo_chunk(l, c, slot):
                    for half in range(2):
                        lo(l, c, slot, half)

                def slice_and_split(l, i, b, c_up, c, slot, tiles=None):
                    square_relu(l, i, tiles or [banks[4 + b][:, :]], c_up)
                    lo(l, c, slot, 0)
                    h_to_lo(l, i, b)
                    lo(l, c, slot, 1)

                lo_chunk(l, FIRST_UP + 1, (FIRST_UP + 1) % RING)
                slice_and_split(l, 0, 0, FIRST_UP, FIRST_UP + 2, (FIRST_UP + 2) % RING,
                                [tile[:, 0:SEQ] for tile in up_0])
                for c in (FIRST_UP + 3, FIRST_UP + 4):
                    lo_chunk(l, c, c % RING)
                with dve.Fori(0, SPLIT_TURNS) as j:
                    for b in range(2):
                        c = FIRST_UP + 5 + 2 * b
                        slice_and_split(l, j * 2 + (1 + b), (1 + b) % 2, j * 4 + (c - 4), j * 4 + c, c % RING)
                        lo_chunk(l, j * 4 + (c + 1), (c + 1) % RING)
                slice_and_split(l, UPS - 3, 1, CHUNKS - 7, CHUNKS - 3, (CHUNKS - 3) % RING)
                lo_chunk(l, CHUNKS - 2, (CHUNKS - 2) % RING)
                slice_and_split(l, UPS - 2, 0, CHUNKS - 5, CHUNKS - 1, (CHUNKS - 1) % RING)
                square_relu(l, UPS - 1, [banks[5][:, :]], CHUNKS - 3)
                h_to_lo(l, UPS - 1, 1)
                dve.wait_ge(rstd_done, l * STATS + ST_M + 1)
                for n in range(2):
                    for t in range(TOK):
                        if (n, t) == (1, 1):
                            dve.wait_ge(weights_used, used(l, UNITS - 1))
                        else:
                            dve.wait_ge(acc_mlp_done, l * 3 + 2 * n + t + 1)
                        add_to_x(acc_d[t][n], t, n, ST_M, x_updated)
            dve.wait_ge(x_updated, 2 * TOK * (DEPTH + 1))

            def final_mean(t):
                dve.wait_ge(summed, DEPTH * STATS + TOK + t + 2)
                dve.scalar_tensor_tensor(out=means[:, ST_X, t:t + 1], in0=sums[:, 0, t:t + 1], scalar=NORM_EPS,
                                         in1=sums[:, 1, t:t + 1], op0=ALU.add, op1=ALU.add)\
                    .then_inc(mean_done, 1)

            def gain_only(n):
                cols = slice(n * BANK, (n + 1) * BANK)
                dve.tensor_tensor((rope_a, rope_b)[n][:, 1, :], x[:, 1, cols], final_gain[:, cols], ALU.mult)\
                    .then_inc(x_gained, 1)

            def gain_and_norm(n):
                cols = slice(n * BANK, (n + 1) * BANK)
                dve.wait_ge(rstd_done, DEPTH * STATS + 1)
                dve.scalar_tensor_tensor(out=x[:, 0, cols], in0=x[:, 0, cols], scalar=rstd[:, ST_X, 0:1],
                                         in1=final_gain[:, cols], op0=ALU.mult, op1=ALU.mult)\
                    .then_inc(final_0, 1)

            final_mean(0)
            dve.wait_ge(final_gain_loaded, 16)
            gain_only(0)
            final_mean(1)
            gain_only(1)
            for n in range(2):
                gain_and_norm(n)

        @block.tensor
        def _(pe):
            pe.sem_inc(weights_used, UNITS_HELD)
            pe.sem_inc(qk_turned, 4)
            pe.sem_inc(p_turned, 2)
            pe.sem_inc(pv_done, 2)
            pe.wait_ge(zeros_set, 1)
            def warm_up(n):
                for _ in range(n):
                    pe.matmul(banks[1][:, 0:P], probs[:, 0, 0:P], probs[:, 0, 0:P], start=True, stop=True)

            warm_up(WARM_UP[0])
            pe.wait_ge(gains_loaded, 32)
            pe.transpose(banks[0][:, 0:n_gains], gain_rows[:, :], ident[0:n_gains, 0:n_gains])\
                .then_inc(gains_turned, 1)
            warm_up(WARM_UP[1])
            pe.wait_ge(gains_kept, 1)

            def unit_ready(l, c, half):
                pe.wait_ge(split_done, l * UNITS + c * 2 + (half + 1 + UNITS_HELD))

            def three(out, s_hi, s_lo, m_hi, m_lo, first, last):
                pe.matmul(out, s_hi, m_hi, start=first, stop=False)
                pe.matmul(out, s_hi, m_lo, start=False, stop=False)
                return pe.matmul(out, s_lo, m_hi, start=False, stop=last)

            def turn(out, src, k):
                for t in range(TOK):
                    last = pe.transpose(out[:, t * P:(t + 1) * P], src[:, t, k * P:(k + 1) * P], ident[:, :])
                return last

            def turn_x(tiles, ks):
                for k in ks:
                    turn(turned_tile(tiles, k), x, k).then_inc(turned, 1)

            def turn_pair(bank, k):
                turn(pair(bank, k), o, k)
                turn(pair(bank, k + 1), o, k + 1).then_inc(turned, 2)

            def project_in(l, s):
                u = s // 2
                g, k = u // 4, u % 4 * 2 + s % 2
                c = u // 2
                cols = slice((k % 4) * BANK, (k % 4 + 1) * BANK)
                if s == 0:
                    pe.wait_ge(first_lo_half, l + 1)
                elif s % 2 == 0 or s == 1:
                    unit_ready(l, c, u % 2)
                if g == 0:
                    pe.wait_ge(turned_lo, l * TRS + TR_X + k + 1)
                if k == 0 and g in (2, 3, 5):
                    pe.wait_ge(rope_terms, l * 8 + 2 * ROPE_GROUPS[g - 2] + 2)
                if k == 0 and g == 4:
                    pe.wait_ge(v_done, l * 2 + 1)
                for t in range(TOK):
                    tok = slice(t * P, (t + 1) * P)
                    last = three(banks[2 * (g % 2) + t][:, :], xt_hi[:, k, tok], xt_lo[:, k, tok],
                                 w_hi[:, c % RING, cols], w_lo[:, c % RING, cols], k == 0, k == KT - 1)
                    if t == TOK - 1 and s % 2 == 1:
                        last.then_inc(weights_used, 1)

            def project_out(l, acc, k, u, t, n, first, last):
                c = u // 2
                cols = slice((u % 2) * UNIT + n * BANK, (u % 2) * UNIT + (n + 1) * BANK)
                tok = slice(t * P, (t + 1) * P)
                return three(acc[t][n][:, :], ot_hi[:, k, tok], ot_lo[:, k, tok],
                             w_hi[:, c % RING, cols], w_lo[:, c % RING, cols], first, last)

            def attention(l, s):
                if s in QKT_AT:
                    n = QKT_AT[s]
                    j = n // 2
                    pe.wait_ge(rope_done, l * 8 + 2 * j + 2)
                    pe.wait_ge(qk_copied, l * 8 + n + 1)
                    pe.wait_ge(p_copied, l * N_HEADS + sum(x_ < s for x_ in PT_AT) + 1)
                    for k in range(2):
                        for t in range(TOK):
                            f = 2 * (n % 2) + k
                            last = pe.transpose(t_bank[:, k * SEQ + t * P:k * SEQ + (t + 1) * P],
                                                roped[:, j % 2, t, f * P:(f + 1) * P], ident[:, :])
                    last.then_inc(qk_turned, 1)
                if s in PT_AT:
                    h = PT_AT[s]
                    pe.wait_ge(exp_done, l * N_HEADS + h + 3)
                    pe.wait_ge(p_copied, l * N_HEADS + h + 1)
                    pe.wait_ge(qk_copied, l * 8 + sum(x_ <= s for x_ in QKT_AT) + 1)
                    for n in range(3):
                        last = pe.transpose(t_bank[:, n * P:(n + 1) * P], probs[:, h % 2, n * P:(n + 1) * P],
                                            ident[:, :])
                    last.then_inc(p_turned, 1)
                if s in PV_AT:
                    h = PV_AT[s]
                    st, hh = h // SET_HEADS, h % SET_HEADS
                    pe.wait_ge(p_copied, l * N_HEADS + h + 2)
                    pe.wait_ge(v_done, l * 2 + st + 1)
                    if h % 4 == 0 and h > 0:
                        pe.wait_ge(o_done, l * 4 + h // 4)
                    cols = slice(hh * HEAD_DIM, (hh + 1) * HEAD_DIM)
                    pt = probs_t[:, h % 2, :]
                    o0 = o_bank[:, h % 4 * HEAD_DIM:(h % 4 + 1) * HEAD_DIM]
                    o1 = o_bank[:, (4 + h % 4) * HEAD_DIM:(5 + h % 4) * HEAD_DIM]
                    pe.matmul(o0, pt[:, 0:P], v[:, st, 0, cols], start=True, stop=True)
                    pe.matmul(o1, pt[:, P:2 * P], v[:, st, 0, cols], start=True, stop=False)
                    pe.matmul(o1, pt[:, 2 * P:3 * P], v[:, st, 1, cols], start=False, stop=True)\
                        .then_inc(pv_done, 1)
                if s in QK_AT:
                    h = QK_AT[s]
                    hh = h % SET_HEADS
                    rows = slice(hh % 2 * HEAD_DIM, (hh % 2 + 1) * HEAD_DIM)
                    if hh % 4 == 0:
                        pe.wait_ge(qk_copied, l * 8 + 4 * (h // SET_HEADS) + hh // 4 + 4)
                    if h == SET_HEADS:
                        pe.wait_ge(turned_lo, l * TRS + TR_D + 4)
                    if hh >= 2:
                        pe.wait_ge(masked, l * N_HEADS + h - 1)
                    bank = s_banks[h % 2]
                    pe.matmul(bank[:, 0:P], q_t[rows, hh // 2, 0:P], k_t[rows, hh // 2, 0:P],
                              start=True, stop=True)
                    pe.matmul(bank[:, P:3 * P], q_t[rows, hh // 2, P:2 * P], k_t[rows, hh // 2, :],
                              start=True, stop=True).then_inc(scored, 1)
                if s == TURN_D:
                    pe.wait_ge(o_done, l * 4 + 2)
                    pe.wait_ge(masked, l * N_HEADS + SET_HEADS)
                    for n in range(2):
                        turn_pair(s_banks[n], 2 * n)
                if s == TURN_A:
                    pe.wait_ge(o_done, l * 4 + 3)
                    pe.wait_ge(masked, l * N_HEADS + N_HEADS)
                    turn_pair(s_banks[0], 0)

            def up_tile(l, c, slot, out, f, k):
                if f == 0 and k % 4 == 0:
                    unit_ready(l, c, k // 4)
                cols = slice(k * SEQ + f * P, k * SEQ + (f + 1) * P)
                last = three(out, w_hi[:, slot, cols], w_lo[:, slot, cols],
                             xt_hi[:, k, :], xt_lo[:, k, :], k == 0, k == KT - 1)
                if f == 1 and k % 4 == 3:
                    last.then_inc(weights_used, 1)

            def up(l, c, slot, bank):
                for f in range(2):
                    for k in range(KT):
                        up_tile(l, c, slot, bank[:, f * SEQ:(f + 1) * SEQ], f, k)

            def down(l, i, c, slot, b, first=False, last=False):
                pe.wait_ge(h_split, l * UPS + i + 1)
                if last:
                    unit_ready(l, c, 1)
                    for n in range(2):
                        for t in range(TOK):
                            for j in range(2):
                                cols = slice(j * UNIT + n * BANK, j * UNIT + (n + 1) * BANK)
                                tok = slice(t * P, (t + 1) * P)
                                mm = three(acc_d[t][n][:, :], h_hi[:, b, j, tok], h_lo[:, b, j, tok],
                                           w_hi[:, slot, cols], w_lo[:, slot, cols], False, j == 1)
                            if (n, t) != (1, 1):
                                mm.then_inc(acc_mlp_done, 1)
                    mm.then_inc(weights_used, 2)
                    return
                for j in range(2):
                    unit_ready(l, c, j)
                    for t in range(TOK):
                        for n in range(2):
                            cols = slice(j * UNIT + n * BANK, j * UNIT + (n + 1) * BANK)
                            tok = slice(t * P, (t + 1) * P)
                            mm = three(acc_d[t][n][:, :], h_hi[:, b, j, tok], h_lo[:, b, j, tok],
                                       w_hi[:, slot, cols], w_lo[:, slot, cols], first and j == 0, False)
                    mm.then_inc(weights_used, 1)

            with pe.Fori(0, DEPTH) as l:
                for s in range(4 * IN_CHUNKS):
                    if s in (0, 2):
                        wait_all(pe, (x_loaded[s // 2], 16), (x_updated, l * 4 + s + 2))
                        if s == 2:
                            pe.wait_ge(turned_lo, l * TRS + TR_X + 4)
                        turn_x(x_banks, range(2 * s, 2 * s + 4))
                    project_in(l, s)
                    attention(l, s)
                pe.wait_ge(rope_terms, l * 8 + 8)
                for u in range(2 * IN_CHUNKS, 2 * IN_CHUNKS + 4, 2):
                    k0 = u - 2 * IN_CHUNKS
                    for t in range(TOK):
                        for k in range(k0, k0 + 2):
                            if t == 0:
                                unit_ready(l, u // 2, k - k0)
                                pe.wait_ge(turned_lo, l * TRS + TR_D + k + 1)
                            elif k == 0:
                                pe.wait_ge(v_done, l * 2 + 2)
                            for n in range(2):
                                mm = project_out(l, acc_d, k, u + k - k0, t, n, k == 0, k == 3)
                            if t == TOK - 1:
                                mm.then_inc(weights_used, 1)
                            attention(l, 2 * u + 2 * t + k - k0)
                attention(l, TAIL)
                u0 = 2 * IN_CHUNKS + 4
                unit_ready(l, u0 // 2, 1)
                pe.wait_ge(turned_lo, l * TRS + TR_A + 2)
                pe.wait_ge(p_copied, l * N_HEADS + N_HEADS + 1)
                for n in range(2):
                    for k in range(2):
                        project_out(l, acc_a, 4 + k, u0 + k, 0, n, k == 0, False)
                    if n == 0:
                        pe.wait_ge(o_done, l * 4 + 4)
                        turn_pair(s_banks[1], 2)
                for n in (1, 0):
                    if n == 0:
                        pe.wait_ge(turned_lo, l * TRS + TR_A + 4)
                    for k in range(2):
                        mm = project_out(l, acc_a, 4 + k, u0 + k, 1, n, k == 0, False)
                        if n == 0:
                            mm.then_inc(weights_used, 1)
                unit_ready(l, u0 // 2 + 1, 1)
                for n in range(2):
                    for t in range(TOK):
                        if (n, t) == (1, 1):
                            pe.wait_ge(x_mid, l * 4 + 2)
                            turn_x(m_banks, range(4))
                        for k in range(2, 4):
                            mm = project_out(l, acc_a, 4 + k, u0 + k, t, n, False, k == 3)
                        if (n, t) != (1, 1):
                            mm.then_inc(acc_a_done, 1)
                mm.then_inc(weights_used, 2)
                for k in range(KT):
                    if k == 2:
                        pe.wait_ge(x_mid, l * 4 + 4)
                        pe.wait_ge(turned_lo, l * TRS + TR_M + 4)
                        turn_x(m_banks, range(4, KT))
                    pe.wait_ge(turned_lo, l * TRS + TR_M + k + 1)
                    for f in range(2):
                        up_tile(l, FIRST_UP, FIRST_UP % RING, up_0[f][:, 0:SEQ], f, k)
                up(l, FIRST_UP + 1, 1, banks[5])
                down(l, 0, FIRST_UP + 2, 2, 0, first=True)
                with pe.Fori(0, MLP_TURNS) as j:
                    c = j * 4 + (FIRST_UP + 3)
                    up(l, c, 3, banks[4])
                    down(l, j * 2 + 1, c + 1, 0, 1)
                    up(l, c + 2, 1, banks[5])
                    down(l, j * 2 + 2, c + 3, 2, 0)
                down(l, UPS - 1, CHUNKS - 1, (CHUNKS - 1) % RING, 1, last=True)


def shape_constants():
    ident = np.eye(P, dtype=np.float32)
    inv = (1.0 / ROPE_THETA ** (np.arange(0, HEAD_DIM, 2, dtype=np.float64) / HEAD_DIM)).astype(np.float32)
    ang = (np.arange(SEQ, dtype=np.float32)[:, None] * inv[None, :]).astype(np.float64)
    rope = np.concatenate([np.cos(ang), np.sin(ang), -np.sin(ang)], axis=1).astype(np.float32)
    rope = np.ascontiguousarray(rope.reshape(TOK, P, 3 * HALF).transpose(1, 0, 2))
    d = np.arange(P)[:, None] - np.arange(2 * P)[None, :] + P
    counts = sum(((d <= w) & (d % r == 0)).astype(np.int64) for w, r in DILATED_CONFIGS)
    dilated = np.where((d >= 0) & (counts > 0), np.log(np.maximum(counts, 1)) / SCALE, NEG_INF)
    causal = np.where(d >= 0, 0.0, NEG_INF)
    masks = np.ascontiguousarray(np.stack([dilated, causal], axis=1).astype(np.float32))
    return ident, masks, rope


_INS = ["x", "w_in", "w_out", "w_up", "w_down", "final_norm"]


def kernel(**inputs):
    import numpy as _np
    import concourse.bacc as _bacc
    from concourse import mybir as _mybir
    from concourse.bass_utils import run_bass_kernel_spmd as _run

    nc = _bacc.Bacc("TRN2", target_bir_lowering=False, num_devices=1)
    arrays = {f"in_{name}": _np.ascontiguousarray(inputs[name]) for name in _INS}
    arrays["in_gain_rows"] = _np.concatenate(
        [_np.asarray(inputs[name])[l].reshape(-1, P) for l in range(DEPTH)
         for name in ("attn_norm", "mlp_norm", "moba_out_norm", "dil_out_norm")])
    arrays |= dict(zip(("c_ident", "c_masks", "c_rope"), shape_constants()))
    args = [nc.dram_tensor(n, a.shape, _mybir.dt.from_np(a.dtype), kind="ExternalInput").ap()
            for n, a in arrays.items()]
    args.append(nc.dram_tensor("out", (1, SEQ, D_MODEL), _mybir.dt.float32, kind="ExternalOutput").ap())
    hybrid_kernel(nc, *args)
    r = _run(nc, [arrays], core_ids=[0])
    return r.results[0]["out"]
```
